# Optimizing a Trainium2 kernel written in Bass

```python
import math
import jax, jax.numpy as jnp
from jax import lax
import numpy as np

D_MODEL = 2048
BATCH = 1
SEQ = 256
DEPTH = 1

RET_HEADS = 8
RET_DK = 128
RET_DV = 256
RET_CHUNK = 128
POOL_WINDOWS = (2, 4, 8, 16)
POOL_GROUPS = len(POOL_WINDOWS)
POOL_DIM = 1024
POOL_GDIM = POOL_DIM // POOL_GROUPS
N_BRANCH = 2
PEER_HEADS = 8
PEER_NKEYS = 128
PEER_N_EXPERTS = PEER_NKEYS * PEER_NKEYS
PEER_DKEY = 256
PEER_DHALF = PEER_DKEY // 2
PEER_TOPK = 16
PEER_BLOCK = 128

ROPE_BASE = 10000.0
EPS = 1e-6

Q_DIM = RET_HEADS * RET_DK
V_DIM = RET_HEADS * RET_DV
SPLITS = (Q_DIM, Q_DIM, V_DIM, V_DIM, POOL_DIM, N_BRANCH * D_MODEL)
IN_COLS = sum(SPLITS)

kernel_name = "hybrid_retention_pool_peer_block"

def rmsnorm(x, w):
    xf = x.astype(jnp.float32)
    y = xf * lax.rsqrt(jnp.mean(xf * xf, axis=-1, keepdims=True) + EPS)
    return (y * w.astype(jnp.float32)).astype(x.dtype)

def rotary(x):
    S, d = x.shape[1], x.shape[-1]
    half = d // 2
    inv_freq = ROPE_BASE ** (-jnp.arange(half, dtype=jnp.float32) / half)
    ang = jnp.arange(S, dtype=jnp.float32)[:, None] * inv_freq[None, :]
    cos = jnp.cos(ang)[None, :, None, :]
    sin = jnp.sin(ang)[None, :, None, :]
    xf = x.astype(jnp.float32)
    x1, x2 = xf[..., :half], xf[..., half:]
    out = jnp.concatenate([x1 * cos - x2 * sin, x1 * sin + x2 * cos], axis=-1)
    return out.astype(x.dtype)

def retention_chunkwise(q, k, v):
    B, S, H, dk = q.shape
    dv = v.shape[-1]
    C = RET_CHUNK
    N = S // C
    log_g = jnp.log(1.0 - 2.0 ** (-5.0 - jnp.arange(H, dtype=jnp.float32)))
    i = jnp.arange(C, dtype=jnp.float32)
    diff = i[:, None] - i[None, :]
    dmask = jnp.where(diff[None] >= 0,
                      jnp.exp(log_g[:, None, None] * jnp.maximum(diff, 0.0)[None]), 0.0)
    xi = jnp.exp(log_g[None, :] * (i[:, None] + 1.0))
    zeta = jnp.exp(log_g[None, :] * (C - 1.0 - i)[:, None])
    g_chunk = jnp.exp(log_g * C)

    qc = q.reshape(B, N, C, H, dk).astype(jnp.float32)
    kc = k.reshape(B, N, C, H, dk).astype(jnp.float32)
    vc = v.reshape(B, N, C, H, dv).astype(jnp.float32)

    scores = jnp.einsum('bnihd,bnjhd->bnhij', qc, kc) * dmask[None, None]
    inner = jnp.einsum('bnhij,bnjhe->bnihe', scores, vc)

    qx = jnp.moveaxis(qc * xi[None, None, :, :, None], 1, 0)
    kz = jnp.moveaxis(kc * zeta[None, None, :, :, None], 1, 0)
    vn = jnp.moveaxis(vc, 1, 0)

    def step(R, inp):
        qi, ki, vi = inp
        cross = jnp.einsum('bihd,bhde->bihe', qi, R)
        R = g_chunk[None, :, None, None] * R + jnp.einsum('bjhd,bjhe->bhde', ki, vi)
        return R, cross

    R0 = jnp.zeros((B, H, dk, dv), jnp.float32)
    _, cross = lax.scan(step, R0, (qx, kz, vn))
    out = inner + jnp.moveaxis(cross, 0, 1)
    return out.reshape(B, S, H, dv)

def head_groupnorm(y):
    mu = jnp.mean(y, axis=-1, keepdims=True)
    var = jnp.mean((y - mu) ** 2, axis=-1, keepdims=True)
    return (y - mu) * lax.rsqrt(var + EPS)

def multiscale_pool(p):
    B, S, _ = p.shape
    pf = p.astype(jnp.float32)
    cs = jnp.cumsum(pf, axis=1)
    pos = jnp.arange(S, dtype=jnp.int32)
    outs = []
    for g, w in enumerate(POOL_WINDOWS):
        sl = slice(g * POOL_GDIM, (g + 1) * POOL_GDIM)
        csg = cs[..., sl]
        shifted = jnp.pad(csg, ((0, 0), (w, 0), (0, 0)))[:, :S]
        count = jnp.minimum(pos + 1, w).astype(jnp.float32)
        mean = (csg - shifted) / count[None, :, None]
        outs.append(mean - pf[..., sl])
    return jnp.stack(outs, axis=2).astype(p.dtype)

def peer_ffn(h, w_q, sub_keys, u, v):
    B, S, D = h.shape
    T = B * S
    xs = h.reshape(T // PEER_BLOCK, PEER_BLOCK, D)

    def block(xb):
        q = (xb @ w_q).reshape(PEER_BLOCK, PEER_HEADS, 2, PEER_DHALF)
        s = jnp.einsum('thpd,pkd->thpk', q, sub_keys).astype(jnp.float32)
        sv, si = lax.top_k(s, PEER_TOPK)
        cand = (sv[:, :, 0, :, None] + sv[:, :, 1, None, :]).reshape(PEER_BLOCK, PEER_HEADS, -1)
        cidx = (si[:, :, 0, :, None] * PEER_NKEYS + si[:, :, 1, None, :]).reshape(PEER_BLOCK, PEER_HEADS, -1)
        best, pos = lax.top_k(cand, PEER_TOPK)
        eidx = jnp.take_along_axis(cidx, pos, axis=-1)
        gate = jax.nn.softmax(best, axis=-1)
        u_sel = u[eidx]
        v_sel = v[eidx]
        a = jnp.einsum('thkd,td->thk', u_sel, xb).astype(jnp.float32)
        wgt = (jax.nn.gelu(a, approximate=False) * gate).astype(xb.dtype)
        return jnp.einsum('thk,thkd->td', wgt, v_sel)

    y = lax.map(block, xs)
    return y.reshape(B, S, D)

def setup_inputs(seed: int = 0) -> dict:
    key = jax.random.key(seed)
    ks = jax.random.split(key, 16)
    f32 = jnp.float32
    nrm = lambda k, shape, scale: jax.random.normal(k, shape, f32) * scale
    return {
        "x": nrm(ks[0], (BATCH, SEQ, D_MODEL), 1.0),
        "norm1_w": 1.0 + nrm(ks[1], (DEPTH, D_MODEL), 0.02),
        "w_in": nrm(ks[2], (DEPTH, D_MODEL, IN_COLS), D_MODEL ** -0.5),
        "w_ret_o": nrm(ks[3], (DEPTH, V_DIM, D_MODEL), V_DIM ** -0.5),
        "w_pool_lin": nrm(ks[4], (DEPTH, POOL_GROUPS, POOL_GDIM, POOL_GDIM), POOL_GDIM ** -0.5),
        "pool_scale": 1.0 + nrm(ks[5], (DEPTH, POOL_DIM), 0.1),
        "w_pool_o": nrm(ks[6], (DEPTH, POOL_DIM, D_MODEL), POOL_DIM ** -0.5),
        "w_out": nrm(ks[7], (DEPTH, D_MODEL, D_MODEL), D_MODEL ** -0.5),
        "norm2_w": 1.0 + nrm(ks[8], (DEPTH, D_MODEL), 0.02),
        "peer_w_q": nrm(ks[9], (DEPTH, D_MODEL, PEER_HEADS * PEER_DKEY), D_MODEL ** -0.5),
        "peer_sub_keys": nrm(ks[10], (DEPTH, 2, PEER_NKEYS, PEER_DHALF), PEER_DHALF ** -0.5),
        "peer_u": nrm(ks[11], (DEPTH, PEER_N_EXPERTS, D_MODEL), D_MODEL ** -0.5),
        "peer_v": nrm(ks[12], (DEPTH, PEER_N_EXPERTS, D_MODEL), 0.5),
        "final_norm_w": 1.0 + nrm(ks[13], (D_MODEL,), 0.02),
    }

def reference(x, norm1_w, w_in, w_ret_o, w_pool_lin, pool_scale, w_pool_o, w_out,
              norm2_w, peer_w_q, peer_sub_keys, peer_u, peer_v, final_norm_w):
    B, S, D = x.shape
    offsets = np.cumsum(SPLITS)[:-1].tolist()
    for l in range(DEPTH):
        h = rmsnorm(x, norm1_w[l])
        proj = h @ w_in[l]
        q, k, vr, gr, pin, gates = jnp.split(proj, offsets, axis=-1)
        q = rotary(q.reshape(B, S, RET_HEADS, RET_DK))
        k = rotary(k.reshape(B, S, RET_HEADS, RET_DK)) * (RET_DK ** -0.5)
        vr = vr.reshape(B, S, RET_HEADS, RET_DV)
        ret = head_groupnorm(retention_chunkwise(q, k, vr)).reshape(B, S, V_DIM)
        ret = (jax.nn.silu(gr.astype(jnp.float32)) * ret).astype(x.dtype)
        y_ret = ret @ w_ret_o[l]

        pooled = multiscale_pool(pin)
        pooled = jnp.einsum('bsgc,gcd->bsgd', pooled, w_pool_lin[l]).reshape(B, S, POOL_DIM)
        y_pool = (pooled * pool_scale[l]) @ w_pool_o[l]

        g_ret, g_pool = jnp.split(jax.nn.sigmoid(gates.astype(jnp.float32)), 2, axis=-1)
        mixed = (g_ret * y_ret + g_pool * y_pool).astype(x.dtype)
        x = x + mixed @ w_out[l]
        h2 = rmsnorm(x, norm2_w[l])
        x = x + peer_ffn(h2, peer_w_q[l], peer_sub_keys[l], peer_u[l], peer_v[l])
    return rmsnorm(x, final_norm_w)


_drawn_inputs = setup_inputs


def setup_inputs(seed=0):
    import zlib

    import numpy as np

    out = dict(_drawn_inputs(seed))
    spreads = {}
    factors = {}
    for name, (base, spread) in spreads.items():
        noise = np.random.default_rng([zlib.crc32(name.encode()), seed]).standard_normal(out[name].shape)
        drawn = base * np.exp(spread * noise) if base else spread * noise
        out[name] = __import__('jax').numpy.asarray(drawn.astype(out[name].dtype))
    for name, factor in factors.items():
        out[name] = (out[name] * factor).astype(out[name].dtype)
    return out
```

```python
from contextlib import ExitStack

import numpy as np

import concourse.bass as bass
from concourse import mybir

F32 = mybir.dt.float32
F32R = mybir.dt.float32r
U32 = mybir.dt.uint32
ALU = mybir.AluOpType
ACT = mybir.ActivationFunctionType
AX_X = mybir.AxisListType.X

P = 128
D = 2048
SEQ = 256
NB = SEQ // P
KC = D // P
HEADS, DK, DV = 8, 128, 256
Q_DIM, V_DIM = HEADS * DK, HEADS * DV
POOL_WINDOWS = (2, 4, 8, 16)
POOL_GROUPS, POOL_DIM = len(POOL_WINDOWS), 1024
POOL_GDIM = POOL_DIM // POOL_GROUPS
POOL_KC = POOL_DIM // P
PEER_HEADS, NKEYS, TOPK = 8, 128, 16
EPS = 1e-6
ROPE_BASE = 10000.0
NEG = -3.0e38

SLAB = 1024
HALF = 512
BANKS = NB * (SLAB // HALF)

Q0, K0, V0 = 0, Q_DIM, 2 * Q_DIM
G0 = V0 + V_DIM
P0 = G0 + V_DIM
GATE0 = P0 + POOL_DIM
MIX_COLS = GATE0
MIX_SLABS = MIX_COLS // SLAB
GATE_SLABS = 2 * D // SLAB
D_SLABS = D // SLAB
S_MIX = 0
S_GATE = S_MIX + MIX_SLABS
S_RET = S_GATE + GATE_SLABS
S_POOL = S_RET + D_SLABS
S_OUT = S_POOL + D_SLABS
S_Q = S_OUT + D_SLABS
S_END = S_Q + D_SLABS


def first_tile(slab):
    short = min(max(slab - S_POOL, 0), D_SLABS)
    return slab * KC - short * (KC - POOL_KC)


TILES = first_tile(S_END)
W_RING = 4
GATHER_RING = 4
UNITS = NB * PEER_HEADS
HEADS_PER_SLAB = SLAB // (2 * NKEYS)
QUARTER = HEADS_PER_SLAB

A_MASK = NB * MIX_COLS
A_BAND = A_MASK + HEADS * SEQ
A_WLIN = A_BAND + POOL_GROUPS * NB * SEQ
ARENA = A_WLIN + POOL_GROUPS * 2 * POOL_GDIM
A_URING = NB * D
A_VRING = A_URING + GATHER_RING * D
assert A_VRING + GATHER_RING * D <= ARENA


def constants():
    half = DK // 2
    inv_freq = (ROPE_BASE ** (-np.arange(half, dtype=np.float32) / half)).astype(np.float32)
    ang = np.arange(SEQ, dtype=np.float32)[:, None] * inv_freq[None, :]
    rope = np.stack([np.cos(ang), np.sin(ang)], 1).astype(np.float32)
    log_g = np.log(1.0 - 2.0 ** (-5.0 - np.arange(HEADS, dtype=np.float64)))
    diff = np.arange(SEQ)[None, :] - np.arange(P)[:, None]
    decay = np.where(diff[:, None] >= 0, np.exp(log_g[None, :, None] * np.maximum(diff, 0)[:, None]), 0.0)
    decay = decay * DK ** -0.5
    mask = decay.astype(np.float32)
    band = np.zeros((NB, P, POOL_GROUPS, SEQ), np.float32)
    for g, w in enumerate(POOL_WINDOWS):
        for t in range(SEQ):
            lo = max(0, t - w + 1)
            for s in range(lo, t + 1):
                band[s // P, s % P, g, t] = 1.0 / (t + 1 - lo) - (1.0 if s == t else 0.0)
    band = np.ascontiguousarray(band.transpose(1, 2, 0, 3))
    return {
        "rope": rope,
        "mask": mask.reshape(P, -1),
        "band": band.reshape(P, -1),
        "ident": np.eye(P, dtype=np.float32),
        "iota": np.tile(np.arange(TOPK, dtype=np.float32), (P, 1)),
    }


def build(nc, a, out):
    with ExitStack() as ctx:
        def sb(name, shape, dt=F32):
            return ctx.enter_context(nc.sbuf_tensor(name, shape, dt))

        def sem(name):
            return ctx.enter_context(nc.semaphore(name))

        act_hi = sb("act_hi", [P, KC, SEQ], F32R)
        act_lo = sb("act_lo", [P, KC, SEQ], F32R)
        pact_hi = sb("pact_hi", [P, POOL_KC, SEQ], F32R)
        pact_lo = sb("pact_lo", [P, POOL_KC, SEQ], F32R)
        w_hi = sb("w_hi", [P, W_RING, SLAB], F32R)
        w_lo = sb("w_lo", [P, W_RING, SLAB], F32R)
        w_raw = sb("w_raw", [P, W_RING, SLAB])
        x_sb = sb("x_sb", [P, NB, D])
        arena = sb("arena", [P, ARENA])
        rope_gate = sb("rope_gate", [P, 256])
        ident = sb("ident_sb", [P, P])
        iota = sb("iota_sb", [P, TOPK])
        pscale = sb("pscale_sb", [P, POOL_KC])
        keys_hi = sb("keys_hi", [P, 2, NKEYS], F32R)
        keys_lo = sb("keys_lo", [P, 2, NKEYS], F32R)
        qk_tmp = sb("qk_tmp", [P, 1024])
        probs_diag = sb("probs_diag", [P, 768])
        stat = sb("stat", [P, 2 * HEADS, 6])
        mean_var = sb("mean_var", [P, 2 * HEADS, 2])
        norm_a = sb("norm_a", [P, 2 * HEADS])
        norm_b = sb("norm_b", [P, 2 * HEADS])
        norm_c = sb("norm_c", [P, 2 * HEADS])
        top_val = sb("top_val", [P, 2, TOPK])
        top_idx = sb("top_idx", [P, 2, TOPK], U32)
        best = sb("best", [P, TOPK])
        best_pos = sb("best_pos", [P, TOPK], U32)
        pos_ab = sb("pos_ab", [P, 2, TOPK], U32)
        expert_ab = sb("expert_ab", [P, 2, TOPK])
        expert = sb("expert", [P, UNITS, TOPK], U32)
        idx = sb("idx", [P, 3, TOPK], U32)
        dots = sb("dots", [P, TOPK])
        gelu = sb("gelu", [P, TOPK])
        gate_sum = sb("gate_sum", [P, 2])
        weight = sb("weight", [P, TOPK])

        rope = rope_gate[:, :].rearrange("p (t c f) -> p t c f", t=NB, c=2)
        gate = rope_gate[:, :].rearrange("p (u k) -> p u k", u=UNITS)
        keys_raw = expert[:, :, :].bitcast(F32).rearrange("p u k -> p (u k)").rearrange("p (h k) -> p h k", h=2)
        qk_t = qk_tmp[:, :].rearrange("p (r n t) -> p r n t", r=2, n=4)
        tmp_a, tmp_b = qk_tmp[:, 0:512], qk_tmp[:, 512:768]
        key_score = qk_tmp[:, 768:1024]
        probs = probs_diag[:, :].rearrange("p (r t) -> p r t", r=2)
        diag = probs_diag[:, 0:4 * P].rearrange("p (r t) -> p r t", r=4)
        zeros = probs_diag[:, 4 * P:5 * P]
        rows = arena[:, 0:NB * MIX_COLS].rearrange("p (t c) -> p t c", t=NB)
        mask = arena[:, A_MASK:A_BAND].rearrange("p (h c) -> p h c", h=HEADS)
        band = arena[:, A_BAND:A_WLIN].rearrange("p (g s t) -> p g s t", g=POOL_GROUPS, s=NB)
        w_lin = arena[:, A_WLIN:ARENA].rearrange("p (g c d) -> p g c d", g=POOL_GROUPS, c=2)
        h_rows = rows[:, :, 0:D]
        norm1 = rows[:, 0, D:2 * D]
        norm2 = arena[:, A_WLIN:A_WLIN + D]
        h2 = arena[:, 0:NB * D].rearrange("p (t c) -> p t c", t=NB)
        u_ring = arena[:, A_URING:A_VRING].rearrange("p (r c) -> p r c", r=GATHER_RING)
        v_ring = arena[:, A_VRING:A_VRING + GATHER_RING * D].rearrange("p (r c) -> p r c", r=GATHER_RING)
        junk = arena[:, A_URING:A_URING + D]
        q_rows = (junk.rearrange("p (t c) -> p t c", t=NB), w_raw[:, 0:2, :])
        pooled = rows[:, 0, 0:2 * SLAB].rearrange("p (k t) -> p k t", k=POOL_KC)
        rope_tmp = rows[:, 0, G0:G0 + 2 * SLAB]
        final_w = w_raw[:, 2:4, :].rearrange("p r c -> p (r c)")

        bank = ctx.enter_context(nc.psum_tensor("bank", [P, BANKS, HALF], F32))
        misc = ctx.enter_context(nc.psum_tensor("misc", [P, 4, HALF], F32))
        scores_all = misc[:, :, :].rearrange("p b c -> p (b c)")

        x_landed = sem("x_landed")
        norm1_landed = sem("norm1_landed")
        const_landed = sem("const_landed")
        norm2_landed = sem("norm2_landed")
        final_landed = sem("final_landed")
        tile_landed = [sem(f"tile_landed{s}") for s in range(W_RING)]
        tile_hi = sem("tile_hi")
        tile_lo = sem("tile_lo")
        split_free = sem("split_free")
        bank_full = sem("bank_full")
        bank_free = sem("bank_free")
        squares_done = sem("squares_done")
        norm_step = sem("norm_step")
        root_done = sem("root_done")
        rows_ready = sem("rows_ready")
        turned = sem("turned")
        turned_hi = sem("turned_hi")
        turned_lo = sem("turned_lo")
        rope_done = sem("rope_done")
        qk_turned = sem("qk_turned")
        qk_copied = sem("qk_copied")
        scores_full = sem("scores_full")
        probs_ready = sem("probs_ready")
        y_full = sem("y_full")
        y_copied = sem("y_copied")
        pooled_full = sem("pooled_full")
        pooled_copied = sem("pooled_copied")
        lin_full = sem("lin_full")
        lin_hi = sem("lin_hi")
        lin_lo = sem("lin_lo")
        silu_done = sem("silu_done")
        y_normed = sem("y_normed")
        ret_ready = sem("ret_ready")
        pool_gated = sem("pool_gated")
        mixed_ready = sem("mixed_ready")
        resid_ready = sem("resid_ready")
        keys_hi_done = sem("keys_hi_done")
        keys_split = sem("keys_split")
        q_turned = sem("q_turned")
        q_hi = sem("q_hi")
        q_lo = sem("q_lo")
        key_scores = sem("key_scores")
        topk_done = sem("topk_done")
        exp_done = sem("exp_done")
        u_landed = [sem(f"u_landed{s}") for s in range(GATHER_RING)]
        v_landed = [sem(f"v_landed{s}") for s in range(GATHER_RING)]
        u_free = sem("u_free")
        v_free = sem("v_free")
        idx_copied = sem("idx_copied")
        dots_ready = sem("dots_ready")
        gelu_ready = sem("gelu_ready")
        weight_ready = sem("weight_ready")
        diag_ready = sem("diag_ready")
        y_peer_full = sem("y_peer_full")
        zeros_ready = sem("zeros_ready")
        dve_step = sem("dve_step")
        act_step = sem("act_step")
        pool_step = sem("pool_step")
        final_ready = sem("final_ready")
        dve_passed = sem("dve_passed")
        pool_passed = sem("pool_passed")
        stored = sem("stored")

        V_AHEAD = 2 * TOPK

        const_loads = [
            (keys_raw, a["peer_sub_keys"].rearrange("d (p k) -> d p k", p=2)),
            (rope, a["rope"].rearrange("(t p) c f -> p t c f", p=P)),
            (iota[:, :], a["iota"]),
            (pscale[:, :], a["pool_scale"]),
            (arena[:, A_MASK:A_BAND], a["mask"]),
            (arena[:, A_BAND:A_WLIN], a["band"]),
            (w_lin, a["w_pool_lin"].rearrange("g (c p) d -> p g c d", p=P)),
        ]
        CONSTS = 16 * len(const_loads)

        class Steps:

            def __init__(self, eng, semaphore, base=0, apart=None):
                self.eng, self.sem, self.base, self.n, self.apart = eng, semaphore, base, 0, apart

            def __call__(self, ins):
                self.n += 1
                ins.then_inc(self.sem, 1)
                self.eng.wait_ge(self.sem, self.base + self.n)
                if self.apart is not None:
                    self.eng.sem_inc(self.apart, 1)

        block = ctx.enter_context(nc.Block())

        @block.sync
        def _(sp):
            sp.dma_start(x_sb[:, :, :], a["x"].rearrange("(t p) d -> p t d", p=P)).then_inc(x_landed, 16)
            sp.dma_start(norm1, a["norm1_w"].rearrange("(o d) -> o d", o=1).to_broadcast([P, D])).then_inc(norm1_landed, 16)

            def slab_tiles(w, col, t0, kc):
                for k in range(kc):
                    if not (isinstance(t0, int) and t0 + k < W_RING):
                        sp.wait_ge(tile_lo, t0 + (k + 1 - W_RING))
                    sp.dma_start(w_raw[:, k % W_RING, :], w[k * P:(k + 1) * P, bass.ds(col, SLAB)])\
                        .then_inc(tile_landed[k % W_RING], 16)

            sp.dma_start(ident[:, :], a["ident"]).then_inc(x_landed, 16)
            slab_tiles(a["w_in"], 0, 0, KC)
            for dst, src in const_loads:
                sp.dma_start(dst, src).then_inc(const_landed, 16)
            with sp.Fori(1, MIX_SLABS + GATE_SLABS) as j:
                slab_tiles(a["w_in"], j * SLAB, j * KC, KC)
            with sp.Fori(0, D_SLABS) as j:
                slab_tiles(a["w_ret_o"], j * SLAB, first_tile(S_RET) + j * KC, KC)
            sp.wait_ge(lin_full, POOL_GROUPS)
            sp.dma_start(norm2, a["norm2_w"].rearrange("(o d) -> o d", o=1).to_broadcast([P, D])).then_inc(norm2_landed, 16)
            with sp.Fori(0, D_SLABS) as j:
                slab_tiles(a["w_pool_o"], j * SLAB, first_tile(S_POOL) + j * POOL_KC, POOL_KC)
            with sp.Fori(0, D_SLABS) as j:
                slab_tiles(a["w_out"], j * SLAB, first_tile(S_OUT) + j * KC, KC)
            with sp.Fori(0, D_SLABS) as j:
                slab_tiles(a["peer_w_q"], j * SLAB, first_tile(S_Q) + j * KC, KC)
            sp.wait_ge(tile_lo, TILES)
            sp.dma_start(final_w, a["final_norm_w"].rearrange("(o d) -> o d", o=1).to_broadcast([P, D])).then_inc(final_landed, 16)
            for b in range(NB):
                sp.wait_ge(final_ready, b + 1)
                sp.dma_start(out[b * P:(b + 1) * P, :], h2[:, b, :]).then_inc(stored, 16)
            sp.wait_ge(stored, 16 * NB)

        @block.tensor
        def _(pe):
            pe.sem_inc(split_free, W_RING)
            pe.sem_inc(v_free, GATHER_RING + V_AHEAD)

            def slab(s, t0, kc, hi, lo):
                for k in range(kc):
                    r = k % W_RING
                    pe.wait_ge(tile_lo, t0 + k + 1)
                    for t in range(NB):
                        for h in range(2):
                            b = 2 * t + h
                            if k == 0:
                                pe.wait_ge(bank_free, 4 * s + b + 1)
                            o = bank[:, b, :]
                            rh, rl = w_hi[:, r, h * HALF:(h + 1) * HALF], w_lo[:, r, h * HALF:(h + 1) * HALF]
                            lh, ll = hi[:, k, t * P:(t + 1) * P], lo[:, k, t * P:(t + 1) * P]
                            pe.matmul(o, lh, rh, start=(k == 0), stop=False)
                            pe.matmul(o, lh, rl, start=False, stop=False)
                            m = pe.matmul(o, ll, rh, start=False, stop=(k == kc - 1))
                            if k == kc - 1:
                                m.then_inc(bank_full, 1)
                    (pe.drain() if k == kc - 1 else m).then_inc(split_free, 1)

            def turn(stage, src, ready):
                for f in range(8):
                    j, t, h = f // 4, (f // 2) % 2, f % 2
                    for s, n in ready(f):
                        pe.wait_ge(s, n)
                    if stage or f >= 4:
                        pe.wait_ge(turned_lo, 8 * stage + f - 3)
                    for c in range(4):
                        col = j * SLAB + h * HALF + c * P
                        m = pe.transpose(misc[:, f % 4, c * P:(c + 1) * P], src[:, t, col:col + P], ident[:, :])
                    m.then_inc(turned, 1)

            pe.wait_ge(x_landed, 32)
            turn(0, h_rows, lambda f: [(rows_ready, (f // 2) % 2 + 1)])
            pe.wait_ge(turned_lo, 8)
            with pe.Fori(0, MIX_SLABS) as j:
                slab(j, j * KC, KC, act_hi, act_lo)

            pe.wait_ge(rope_done, 2 * NB)
            for i in range(HEADS + 2):
                if i < HEADS:
                    h = i
                    if h >= 2:
                        pe.wait_ge(qk_copied, h - 1)
                    for n in range(4):
                        col = (Q0 if n < 2 else K0) + h * DK
                        m = pe.transpose(misc[:, h % 2, n * P:(n + 1) * P], rows[:, n % 2, col:col + DK], ident[:, :])
                    m.then_inc(qk_turned, 1)
                if 1 <= i <= HEADS:
                    h = i - 1
                    pe.wait_ge(qk_copied, h + 1)
                    if h >= 1:
                        pe.wait_ge(probs_ready, h)
                    q = qk_t[:, h % 2, 0:2, :].rearrange("p n t -> p (n t)")
                    pe.matmul(misc[:, 2, 0:2 * P], qk_t[:, h % 2, 2, :], q, start=True, stop=True)
                    pe.matmul(misc[:, 2, 2 * P:3 * P], qk_t[:, h % 2, 3, :], qk_t[:, h % 2, 1, :],
                              start=True, stop=True).then_inc(scores_full, 1)
                if i >= 2:
                    h = i - 2
                    pe.wait_ge(probs_ready, h + 1)
                    if h == 0:
                        pe.wait_ge(bank_free, 4 * MIX_SLABS)
                    else:
                        pe.wait_ge(y_copied, h)
                    v = [rows[:, t, V0 + h * DV:V0 + (h + 1) * DV] for t in range(NB)]
                    pr = probs[:, h % 2, :]
                    pe.matmul(misc[:, 3, 0:DV], pr[:, 0:P], v[0], start=True, stop=True)
                    pe.matmul(misc[:, 3, DV:2 * DV], pr[:, P:2 * P], v[0], start=True, stop=False)
                    pe.matmul(misc[:, 3, DV:2 * DV], pr[:, 2 * P:3 * P], v[1], start=False, stop=True)\
                        .then_inc(y_full, 1)

            pe.wait_ge(const_landed, CONSTS)
            pe.wait_ge(bank_free, 4 * MIX_SLABS + 4)
            pe.wait_ge(y_copied, HEADS)
            for f in range(POOL_GROUPS):
                for c in range(2):
                    col = P0 + (2 * f + c) * P
                    o = misc[:, f, c * SEQ:(c + 1) * SEQ]
                    pe.matmul(o, rows[:, 0, col:col + P], band[:, f, 0, :], start=True, stop=False)
                    m = pe.matmul(o, rows[:, 1, col:col + P], band[:, f, 1, :], start=False, stop=True)
                m.then_inc(pooled_full, 1)
            for f in range(POOL_GROUPS):
                pe.wait_ge(pooled_copied, f + 1)
                for d in range(2):
                    o = misc[:, f, d * SEQ:(d + 1) * SEQ]
                    for c in range(2):
                        m = pe.matmul(o, w_lin[:, f, c, d * P:(d + 1) * P], pooled[:, 2 * f + c, :],
                                      start=(c == 0), stop=(c == 1))
                m.then_inc(lin_full, 1)

            with pe.Fori(S_GATE, S_RET) as j:
                slab(j, j * KC, KC, act_hi, act_lo)

            pe.wait_ge(lin_lo, POOL_GROUPS)
            turn(1, rows[:, :, G0:G0 + D], lambda f: [(ret_ready, (f // 2) % 2 + 1)])
            pe.wait_ge(turned_lo, 16)
            with pe.Fori(0, D_SLABS) as j:
                slab(S_RET + j, first_tile(S_RET) + j * KC, KC, act_hi, act_lo)
            with pe.Fori(0, D_SLABS) as j:
                slab(S_POOL + j, first_tile(S_POOL) + j * POOL_KC, POOL_KC, pact_hi, pact_lo)

            turn(2, rows[:, :, 0:D], lambda f: [(mixed_ready, f + 1)])
            pe.wait_ge(turned_lo, 24)
            with pe.Fori(0, D_SLABS) as j:
                slab(S_OUT + j, first_tile(S_OUT) + j * KC, KC, act_hi, act_lo)

            turn(3, h2, lambda f: [(rows_ready, 2 + (f // 2) % 2 + 1)])
            pe.wait_ge(turned_lo, 32)
            pe.wait_ge(keys_split, 1)
            for j in range(D_SLABS):
                slab(S_Q + j, first_tile(S_Q + j), KC, act_hi, act_lo)
                if j:
                    pe.wait_ge(topk_done, 2 * QUARTER * j)
                for f in range(4):
                    t, g = f // 2, f % 2
                    pe.wait_ge(bank_free, 4 * (S_Q + j) + BANKS + f + 1)
                    for c in range(4):
                        m = pe.transpose(misc[:, f, c * P:(c + 1) * P],
                                         q_rows[j][:, t, (4 * g + c) * P:(4 * g + c + 1) * P], ident[:, :])
                    m.then_inc(q_turned, 1)
                pe.wait_ge(q_lo, 4 * (j + 1))
                for t in range(NB):
                    for c in range(8):
                        o = misc[:, 2 * t + c // 4, (c % 4) * P:(c % 4 + 1) * P]
                        lh, ll = pact_hi[:, c, t * P:(t + 1) * P], pact_lo[:, c, t * P:(t + 1) * P]
                        rh, rl = keys_hi[:, c % 2, :], keys_lo[:, c % 2, :]
                        pe.matmul(o, lh, rh, start=True, stop=False)
                        pe.matmul(o, lh, rl, start=False, stop=False)
                        m = pe.matmul(o, ll, rh, start=False, stop=True)
                    m.then_inc(key_scores, 1)

            pe.wait_ge(zeros_ready, 1)
            pe.wait_ge(bank_free, 4 * S_END + 4)
            pe.wait_ge(topk_done, UNITS)
            for acc in (bank, misc):
                for n in range(4):
                    pe.matmul(acc[:, n, :], zeros, x_sb[:, 0, n * HALF:(n + 1) * HALF], start=True, stop=False,
                              skip_group_check=True)
            for quarter in range(4):
                acc = (bank, misc)[quarter % 2]
                with pe.Fori(quarter * QUARTER, (quarter + 1) * QUARTER) as u:
                    for k in range(TOPK):
                        r = k % GATHER_RING
                        pe.wait_ge(diag_ready, u * TOPK + k + 1)
                        pe.wait_ge(v_landed[r], u * (16 * TOPK // GATHER_RING) + 16 * (k // GATHER_RING + 1))
                        for n in range(4):
                            m = pe.matmul(acc[:, n, :], diag[:, k % GATHER_RING, :], v_ring[:, r, n * HALF:(n + 1) * HALF],
                                          start=False, stop=False, skip_group_check=True)
                        m.then_inc(v_free, 1)
            for acc in (bank, misc):
                for n in range(4):
                    m = pe.matmul(acc[:, n, :], zeros, x_sb[:, 0, n * HALF:(n + 1) * HALF], start=False, stop=True,
                                  skip_group_check=True)
            m.then_inc(y_peer_full, 1)

        @block.scalar
        def _(act):
            act.sem_inc(bank_free, BANKS)
            step = Steps(act, act_step)

            def tiles(t0, n):
                for k in range(n):
                    r = k % W_RING
                    act.wait_ge(split_free, t0 + k + 1)
                    act.wait_ge(tile_landed[r], landed(t0, k))
                    act.activation(w_hi[:, r, :], w_raw[:, r, :], ACT.Copy).then_inc(tile_hi, 1)

            def landed(t0, k):
                return t0 * (16 // W_RING) + 16 * (k // W_RING + 1)

            def turned_high(stage):
                for f in range(8):
                    n = 8 * stage + f + 1
                    j, t, h = f // 4, (f // 2) % 2, f % 2
                    c = (j * SLAB + h * HALF) // P
                    act.wait_ge(turned, n)
                    act.activation(act_hi[:, c:c + 4, t * P:(t + 1) * P],
                                   misc[:, f % 4, :].rearrange("p (c t) -> p c t", c=4), ACT.Copy).then_inc(turned_hi, 1)

            def squares(n0):
                for t in range(NB):
                    step(act.activation(junk, x_sb[:, t, :], ACT.Square, accum_out=norm_a[:, t:t + 1]))
                act.sem_inc(squares_done, 1)
                act.wait_ge(norm_step, n0)
                act.activation(norm_c[:, 0:NB], norm_b[:, 0:NB], ACT.Sqrt).then_inc(root_done, 1)

            act.wait_ge(x_landed, 32)
            squares(1)
            tiles(0, W_RING)
            turned_high(0)
            for first, last in ((0, G0 // SLAB), (G0 // SLAB, MIX_SLABS)):
                if first:
                    act.wait_ge(rope_done, 2 * NB)
                with act.Fori(first, last) as j:
                    tiles(j * KC + W_RING, KC)
                    for b in range(BANKS):
                        act.wait_ge(bank_full, 4 * j + b + 1)
                        act.activation(rows[:, b // 2, bass.ds(j * SLAB + (b % 2) * HALF, HALF)], bank[:, b, :], ACT.Copy)\
                            .then_inc(bank_free, 1)
            for i in range(HEADS + 2):
                if i < HEADS:
                    act.wait_ge(qk_turned, i + 1)
                    if i >= 2:
                        act.wait_ge(scores_full, i - 1)
                    act.activation(qk_t[:, i % 2, :, :].rearrange("p n t -> p (n t)"), misc[:, i % 2, :], ACT.Copy)\
                        .then_inc(qk_copied, 1)
                if i >= 2:
                    h = i - 2
                    act.wait_ge(y_full, h + 1)
                    act.activation(rows[:, :, V0 + h * DV:V0 + (h + 1) * DV],
                                   misc[:, 3, :].rearrange("p (t c) -> p t c", t=NB), ACT.Copy).then_inc(y_copied, 1)
            for f in range(POOL_GROUPS):
                act.wait_ge(pooled_full, f + 1)
                act.activation(pooled[:, 2 * f:2 * f + 2, :].rearrange("p k t -> p (k t)"), misc[:, f, :], ACT.Copy)\
                    .then_inc(pooled_copied, 1)
            for f in range(POOL_GROUPS):
                act.wait_ge(lin_full, f + 1)
                for d in range(2):
                    m = act.activation(pact_hi[:, 2 * f + d, :], misc[:, f, d * SEQ:(d + 1) * SEQ], ACT.Copy,
                                       scale=pscale[:, 2 * f + d:2 * f + d + 1])
                m.then_inc(lin_hi, 1)
            for t in range(NB):
                act.activation(rows[:, t, G0:G0 + V_DIM], rows[:, t, G0:G0 + V_DIM], ACT.Silu).then_inc(silu_done, 1)
            act.wait_ge(norm_step, 2)
            act.activation(norm_c[:, :], norm_b[:, :], ACT.Sqrt).then_inc(root_done, 1)
            act.activation(keys_hi[:, :, :], keys_raw, ACT.Copy).then_inc(keys_hi_done, 1)
            for first, last in ((0, V0 // SLAB), (V0 // SLAB, GATE_SLABS)):
                if first:
                    act.wait_ge(ret_ready, NB)
                with act.Fori(first, last) as j:
                    tiles(j * KC + first_tile(S_GATE) + W_RING, KC)
                    for b in range(BANKS):
                        act.wait_ge(bank_full, 4 * j + (4 * S_GATE + b + 1))
                        act.activation(rows[:, b // 2, bass.ds(j * SLAB + (b % 2) * HALF, HALF)], bank[:, b, :],
                                       ACT.Sigmoid).then_inc(bank_free, 1)
            turned_high(1)
            with act.Fori(0, D_SLABS) as j:
                tiles(j * KC + first_tile(S_RET) + W_RING, KC)
            with act.Fori(0, D_SLABS) as j:
                tiles(j * POOL_KC + first_tile(S_POOL) + W_RING, POOL_KC)
            turned_high(2)
            with act.Fori(0, D_SLABS) as j:
                tiles(j * KC + first_tile(S_OUT) + W_RING, KC)
            act.wait_ge(bank_free, 4 * S_Q + BANKS)
            squares(3)
            turned_high(3)

            def q_copy(j):
                for b in range(BANKS):
                    act.wait_ge(bank_full, 4 * (S_Q + j) + b + 1)
                    act.activation(q_rows[j][:, b // 2, (b % 2) * HALF:(b % 2 + 1) * HALF], bank[:, b, :], ACT.Copy)\
                        .then_inc(bank_free, 1)
                for f in range(4):
                    t, g = f // 2, f % 2
                    act.wait_ge(q_turned, 4 * j + f + 1)
                    act.activation(pact_hi[:, 4 * g:4 * g + 4, t * P:(t + 1) * P],
                                   misc[:, f, :].rearrange("p (c t) -> p c t", c=4), ACT.Copy).then_inc(q_hi, 1)

            def numerators(u0, n):
                act.activation(gate[:, bass.ds(u0, n), :], gate[:, bass.ds(u0, n), :], ACT.Exp).then_inc(exp_done, n)

            tiles(first_tile(S_Q) + W_RING, KC)
            q_copy(0)
            with act.Fori(0, 3) as i:
                act.wait_ge(topk_done, 2 * i + 2)
                numerators(2 * i, 2)
                tiles(i * W_RING + (first_tile(S_Q + 1) + W_RING), W_RING)
            act.wait_ge(topk_done, 8)
            numerators(6, 2)
            q_copy(1)
            act.wait_ge(topk_done, UNITS)
            numerators(8, 8)
            with act.Fori(0, UNITS) as u:
                act.wait_ge(dots_ready, u + 1)
                act.activation(gelu[:, :], dots[:, :], ACT.Gelu).then_inc(gelu_ready, 1)
                act.wait_ge(weight_ready, u + 1)
                for k in range(TOPK):
                    act.wait_ge(v_free, u * TOPK + (V_AHEAD + k + 1))
                    act.activation(diag[:, k % GATHER_RING, :], ident[:, :], ACT.Copy, scale=weight[:, k:k + 1])\
                        .then_inc(diag_ready, 1)
            for b in range(NB):
                act.wait_ge(resid_ready, b + 1)
                step(act.activation(junk, x_sb[:, b, :], ACT.Square, accum_out=norm_a[:, b:b + 1]))
                act.sem_inc(squares_done, 1)
            act.wait_ge(norm_step, 4)
            act.activation(norm_c[:, 0:NB], norm_b[:, 0:NB], ACT.Sqrt).then_inc(root_done, 1)

        @block.vector
        def _(dve):
            dve.sem_inc(u_free, GATHER_RING)
            step = Steps(dve, dve_step)

            def tiles(t0, n):
                for k in range(n):
                    r = k % W_RING
                    dve.wait_ge(tile_hi, t0 + k + 1)
                    dve.tensor_tensor(w_lo[:, r, :], w_raw[:, r, :], w_hi[:, r, :].bitcast(F32), ALU.subtract)\
                        .then_inc(tile_lo, 1)

            def turned_low(stage):
                for f in range(8):
                    n = 8 * stage + f + 1
                    j, t, h = f // 4, (f // 2) % 2, f % 2
                    c = (j * SLAB + h * HALF) // P
                    dve.wait_ge(turned_hi, n)
                    dve.tensor_tensor(act_lo[:, c:c + 4, t * P:(t + 1) * P],
                                      misc[:, f % 4, :].rearrange("p (c t) -> p c t", c=4),
                                      act_hi[:, c:c + 4, t * P:(t + 1) * P].bitcast(F32), ALU.subtract)\
                        .then_inc(turned_lo, 1)

            def inverse_root(n, width):
                dve.sem_inc(norm_step, 1)
                dve.wait_ge(root_done, n)
                a_, b_, c_ = norm_a[:, 0:width], norm_b[:, 0:width], norm_c[:, 0:width]
                step(dve.reciprocal(a_, c_))
                step(dve.tensor_tensor(c_, a_, a_, ALU.mult))
                step(dve.tensor_tensor(c_, c_, b_, ALU.mult))
                step(dve.tensor_scalar(c_, c_, -0.5, 1.5, ALU.mult, ALU.add))
                step(dve.tensor_tensor(a_, a_, c_, ALU.mult))

            def norm_factor(n, n_squares):
                dve.wait_ge(squares_done, n_squares)
                step(dve.tensor_scalar(norm_b[:, 0:NB], norm_a[:, 0:NB], 1.0 / D, EPS, ALU.mult, ALU.add))
                inverse_root(n, NB)

            norm_factor(1, 1)
            dve.wait_ge(norm1_landed, 16)
            for t in range(NB):
                dve.scalar_tensor_tensor(h_rows[:, t, :], x_sb[:, t, :], norm_a[:, t:t + 1], norm1, ALU.mult, ALU.mult)\
                    .then_inc(rows_ready, 1)
            tiles(0, W_RING)
            turned_low(0)
            with dve.Fori(0, MIX_SLABS) as j:
                tiles(j * KC + W_RING, KC)
            dve.wait_ge(const_landed, CONSTS)
            for h in range(HEADS):
                dve.wait_ge(scores_full, h + 1)
                if h >= 2:
                    dve.wait_ge(y_full, h - 1)
                dve.tensor_tensor(probs[:, h % 2, 0:SEQ], misc[:, 2, 0:SEQ], mask[:, h, :], ALU.mult)
                dve.tensor_tensor(probs[:, h % 2, SEQ:SEQ + P], misc[:, 2, SEQ:SEQ + P], mask[:, h, 0:P], ALU.mult)\
                    .then_inc(probs_ready, 1)
            for f in range(POOL_GROUPS):
                dve.wait_ge(lin_hi, f + 1)
                for d in range(2):
                    c = 2 * f + d
                    m = dve.scalar_tensor_tensor(pact_lo[:, c, :], misc[:, f, d * SEQ:(d + 1) * SEQ], pscale[:, c:c + 1],
                                                 pact_hi[:, c, :].bitcast(F32), ALU.mult, ALU.subtract)
                m.then_inc(lin_lo, 1)
            dve.wait_ge(y_copied, HEADS)
            for n in range(2 * HEADS):
                t, h = n // HEADS, n % HEADS
                m = dve.bn_stats(stat[:, n, :], rows[:, t, V0 + h * DV:V0 + (h + 1) * DV])
            step(m)
            for n in range(2 * HEADS):
                m = dve.bn_aggr(mean_var[:, n, :], stat[:, n, :])
            step(m)
            step(dve.tensor_scalar(norm_b[:, :], mean_var[:, :, 1], EPS, None, ALU.add))
            inverse_root(2, 2 * HEADS)
            for t in range(NB):
                for h in range(HEADS):
                    y = rows[:, t, V0 + h * DV:V0 + (h + 1) * DV]
                    n = t * HEADS + h
                    m = dve.tensor_scalar(y, y, mean_var[:, n, 0:1], norm_a[:, n:n + 1], ALU.subtract, ALU.mult)
                m.then_inc(y_normed, 1)
            dve.memset(zeros, 0.0).then_inc(zeros_ready, 1)
            dve.wait_ge(keys_hi_done, 1)
            dve.tensor_tensor(keys_lo[:, :, :], keys_raw, keys_hi[:, :, :].bitcast(F32), ALU.subtract)\
                .then_inc(keys_split, 1)
            with dve.Fori(0, GATE_SLABS) as j:
                tiles(j * KC + first_tile(S_GATE) + W_RING, KC)
            turned_low(1)
            with dve.Fori(0, D_SLABS) as j:
                tiles(j * KC + first_tile(S_RET) + W_RING, KC)
                for b in range(BANKS):
                    dve.wait_ge(bank_full, 4 * j + (4 * S_RET + b + 1))
                    g = rows[:, b // 2, bass.ds(j * SLAB + (b % 2) * HALF, HALF)]
                    dve.tensor_tensor(g, g, bank[:, b, :], ALU.mult).then_inc(bank_free, 1)
            with dve.Fori(0, D_SLABS) as j:
                tiles(j * POOL_KC + first_tile(S_POOL) + W_RING, POOL_KC)
                for b in range(BANKS):
                    dve.wait_ge(bank_full, 4 * j + (4 * S_POOL + b + 1))
                    g = rows[:, b // 2, bass.ds(j * SLAB + (D + (b % 2) * HALF), HALF)]
                    dve.tensor_tensor(g, g, bank[:, b, :], ALU.mult).then_inc(bank_free, 1)
            turned_low(2)
            with dve.Fori(0, D_SLABS) as j:
                tiles(j * KC + first_tile(S_OUT) + W_RING, KC)
                for b in range(BANKS):
                    dve.wait_ge(bank_full, 4 * j + (4 * S_OUT + b + 1))
                    g = x_sb[:, b // 2, bass.ds(j * SLAB + (b % 2) * HALF, HALF)]
                    dve.tensor_tensor(g, g, bank[:, b, :], ALU.add).then_inc(bank_free, 1)
            norm_factor(3, 2)
            dve.wait_ge(norm2_landed, 16)
            dve.wait_ge(turned, 24)
            for t in range(NB):
                dve.scalar_tensor_tensor(h2[:, t, :], x_sb[:, t, :], norm_a[:, t:t + 1], norm2, ALU.mult, ALU.mult)\
                    .then_inc(rows_ready, 1)
            turned_low(3)

            def q_low(j):
                for f in range(4):
                    t, g = f // 2, f % 2
                    dve.wait_ge(q_hi, 4 * j + f + 1)
                    dve.tensor_tensor(pact_lo[:, 4 * g:4 * g + 4, t * P:(t + 1) * P],
                                      misc[:, f, :].rearrange("p (c t) -> p c t", c=4),
                                      pact_hi[:, 4 * g:4 * g + 4, t * P:(t + 1) * P].bitcast(F32), ALU.subtract)\
                        .then_inc(q_lo, 1)

            TOPK_STEPS = 16
            topk_base = step.n

            def two_rounds(st, pairs, work):
                for src, val, pos in pairs:
                    m = dve.max(val[:, 0:8], src)
                st(m)
                for src, val, pos in pairs:
                    dve.max_index(pos[:, 0:8], val[:, 0:8], src)
                for (src, val, pos), w in zip(pairs, work):
                    m = dve.match_replace(w, val[:, 0:8], src, NEG)
                st(m)
                for (src, val, pos), w in zip(pairs, work):
                    m = dve.max(val[:, 8:16], w)
                st(m)
                for (src, val, pos), w in zip(pairs, work):
                    m = dve.max_index(pos[:, 8:16], val[:, 8:16], w)
                st(m)

            def top_experts(slab_no, n, u):
                st = Steps(dve, dve_step, u * TOPK_STEPS + topk_base, dve_passed)
                s = key_score[:, :]
                st(dve.tensor_copy(s, scores_all[:, bass.ds(n * 2 * NKEYS, 2 * NKEYS)]))
                two_rounds(st, [(s[:, p * NKEYS:(p + 1) * NKEYS], top_val[:, p, :], top_idx[:, p, :]) for p in range(2)],
                           [tmp_a[:, p * NKEYS:(p + 1) * NKEYS] for p in range(2)])
                grid = [P, TOPK, TOPK]
                cand = tmp_b[:, 0:TOPK * TOPK]
                st(dve.tensor_tensor(cand.rearrange("p (a b) -> p a b", a=TOPK),
                                     top_val[:, 0, :].unsqueeze(2).to_broadcast(grid),
                                     top_val[:, 1, :].unsqueeze(1).to_broadcast(grid), ALU.add))
                two_rounds(st, [(cand, best[:, :], best_pos[:, :])], [tmp_a[:, 0:TOPK * TOPK]])
                st(dve.tensor_scalar(gate[:, bass.ds(u, 1), :].rearrange("p u k -> p (u k)"), best[:, :], best[:, 0:1], None,
                                     ALU.subtract))
                dve.tensor_single_scalar(pos_ab[:, 0, :], best_pos[:, :], 4, ALU.logical_shift_right)
                st(dve.tensor_single_scalar(pos_ab[:, 1, :], best_pos[:, :], TOPK - 1, ALU.bitwise_and))
                pick = tmp_a[:, :].rearrange("p (h k j) -> p h k j", h=2, k=TOPK)
                for p in range(2):
                    m = dve.tensor_tensor(pick[:, p, :, :], pos_ab[:, p, :].unsqueeze(2).to_broadcast(grid),
                                          iota[:, :].unsqueeze(1).to_broadcast(grid), ALU.is_equal)
                st(m)
                for p in range(2):
                    m = dve.tensor_tensor(pick[:, p, :, :], pick[:, p, :, :],
                                          top_idx[:, p, :].unsqueeze(1).to_broadcast(grid), ALU.mult)
                st(m)
                st(dve.tensor_reduce(expert_ab[:, :, :], pick, AX_X, ALU.add))
                st(dve.scalar_tensor_tensor(expert[:, bass.ds(u, 1), :].rearrange("p u k -> p (u k)"), expert_ab[:, 0, :],
                                            float(NKEYS), expert_ab[:, 1, :], ALU.mult, ALU.add))
                assert st.n <= TOPK_STEPS
                if st.n < TOPK_STEPS:
                    dve.sem_inc(dve_step, TOPK_STEPS - st.n)
                dve.sem_inc(topk_done, 1)

            tiles(first_tile(S_Q) + W_RING, KC)
            q_low(0)
            dve.wait_ge(key_scores, 2)
            with dve.Fori(0, 3) as i:
                for e in range(2):
                    top_experts(0, 2 * i + e, 2 * i + e)
                tiles(i * W_RING + (first_tile(S_Q + 1) + W_RING), W_RING)
            for n in (6, 7):
                top_experts(0, n, n)
            q_low(1)
            dve.wait_ge(key_scores, 4)
            with dve.Fori(0, 8) as n:
                top_experts(1, n, n + 8)

            base = topk_base + UNITS * TOPK_STEPS
            UNIT_STEPS = TOPK + 2
            for quarter in range(4):
                b = quarter % 2
                with dve.Fori(quarter * QUARTER, (quarter + 1) * QUARTER) as u:
                    st = Steps(dve, dve_step, u * UNIT_STEPS + base)
                    for k in range(TOPK):
                        r = k % GATHER_RING
                        dve.wait_ge(u_landed[r], u * (16 * TOPK // GATHER_RING) + 16 * (k // GATHER_RING + 1))
                        st(dve.tensor_tensor_reduce(out=u_ring[:, r, :], in0=u_ring[:, r, :], in1=h2[:, b, :], scale=1.0,
                                                    scalar=0.0, op0=ALU.mult, op1=ALU.add, accum_out=dots[:, k:k + 1]))
                        dve.sem_inc(u_free, 1)
                    dve.sem_inc(dots_ready, 1)
                    g = gate[:, bass.ds(u, 1), :].rearrange("p u k -> p (u k)")
                    dve.wait_ge(exp_done, u + 1)
                    st(dve.tensor_reduce(gate_sum[:, 0:1], g, AX_X, ALU.add))
                    st(dve.reciprocal(gate_sum[:, 1:2], gate_sum[:, 0:1]))
                    dve.wait_ge(gelu_ready, u + 1)
                    dve.wait_ge(diag_ready, u * TOPK)
                    dve.scalar_tensor_tensor(weight[:, :], gelu[:, :], gate_sum[:, 1:2], g, ALU.mult, ALU.mult)\
                        .then_inc(weight_ready, 1)

            step.base, step.n = base + UNITS * UNIT_STEPS, 0
            dve.wait_ge(y_peer_full, 1)
            for b, acc in enumerate((bank, misc)):
                step(dve.tensor_tensor(x_sb[:, b, :], x_sb[:, b, :], acc[:, :, :].rearrange("p b c -> p (b c)"), ALU.add))
                dve.sem_inc(resid_ready, 1)
            norm_factor(4, 4)
            dve.wait_ge(final_landed, 16)
            for b in range(NB):
                dve.scalar_tensor_tensor(h2[:, b, :], x_sb[:, b, :], norm_a[:, b:b + 1], final_w, ALU.mult, ALU.mult)\
                    .then_inc(final_ready, 1)

        @block.gpsimd
        def _(pool):
            step = Steps(pool, pool_step)
            ta = rope_tmp[:, 0:SLAB].rearrange("p (c f) -> p c f", f=DK // 2)
            tb = rope_tmp[:, SLAB:2 * SLAB].rearrange("p (h c f) -> p h c f", c=2, f=DK // 2)
            pool.wait_ge(const_landed, CONSTS)
            for n in range(2):
                pool.wait_ge(bank_free, 4 * (n + 1) + 4)
                for t in range(NB):
                    x = rows[:, t, n * Q_DIM:(n + 1) * Q_DIM]
                    xc = x.rearrange("p (c f) -> p c f", f=DK // 2)
                    xh = x.rearrange("p (h c f) -> p h c f", c=2, f=DK // 2)
                    th = rope_tmp[:, 0:SLAB].rearrange("p (h c f) -> p h c f", c=2, f=DK // 2)
                    full, part = [P, 2 * HEADS, DK // 2], [P, HEADS, DK // 2]
                    cos, sin = rope[:, t, 0, :].unsqueeze(1), rope[:, t, 1, :].unsqueeze(1)
                    pool.tensor_tensor(ta, xc, cos.to_broadcast(full), ALU.mult)
                    pool.tensor_tensor(tb[:, :, 0, :], xh[:, :, 1, :], sin.to_broadcast(part), ALU.mult)
                    step(pool.tensor_tensor(tb[:, :, 1, :], xh[:, :, 0, :], sin.to_broadcast(part), ALU.mult))
                    pool.tensor_tensor(xh[:, :, 0, :], th[:, :, 0, :], tb[:, :, 0, :], ALU.subtract)
                    step(pool.tensor_tensor(xh[:, :, 1, :], th[:, :, 1, :], tb[:, :, 1, :], ALU.add))
                    pool.sem_inc(rope_done, 1)
            pool.wait_ge(silu_done, NB)
            for t in range(NB):
                pool.wait_ge(y_normed, t + 1)
                pool.tensor_tensor(rows[:, t, G0:G0 + V_DIM], rows[:, t, G0:G0 + V_DIM], rows[:, t, V0:V0 + V_DIM], ALU.mult)\
                    .then_inc(ret_ready, 1)
            for f in range(8):
                j, t, h = f // 4, (f // 2) % 2, f % 2
                col = j * SLAB + h * HALF
                pool.wait_ge(bank_free, 4 * (S_POOL + 1) + f + 1)
                pool.tensor_tensor(rows[:, t, col:col + HALF], rows[:, t, col:col + HALF], rows[:, t, D + col:D + col + HALF],
                                   ALU.add).then_inc(mixed_ready, 1)

            def take_idx(u, slot, n):
                pool.wait_ge(topk_done, u + 1)
                pool.wait_ge(v_free, u * TOPK + GATHER_RING)
                pool.tensor_copy(idx[:, slot, :], expert[:, bass.ds(u, 1), :].rearrange("p u k -> p (u k)"))\
                    .then_inc(idx_copied, 1)
                pool.wait_ge(idx_copied, u + 1)

            def gather(table, ring, landed, slot, k):
                pool.indirect_dma_start(
                    out=ring[:, k % GATHER_RING, :], out_offset=None, in_=table,
                    in_offset=bass.IndirectOffsetOnAxis(ap=idx[:, slot, k:k + 1], axis=0),
                ).then_inc(landed[k % GATHER_RING], 16)

            def gather_u(u, slot, k):
                pool.wait_ge(u_free, u * TOPK + k + 1)
                pool.sem_inc(pool_passed, 1)
                gather(a["peer_u"], u_ring, u_landed, slot, k)

            def gather_v(u, slot, k):
                pool.wait_ge(v_free, u * TOPK + (V_AHEAD + k + 1))
                pool.sem_inc(pool_passed, 1)
                gather(a["peer_v"], v_ring, v_landed, slot, k)

            take_idx(0, 0, 0)
            for k in range(TOPK):
                gather_u(0, 0, k)
            with pool.Fori(0, (UNITS - 1) // 3) as i:
                for m in range(3):
                    take_idx(3 * i + m + 1, (m + 1) % 3, 0)
                    for k in range(TOPK):
                        gather_u(3 * i + m + 1, (m + 1) % 3, k)
                        gather_v(3 * i + m, m, k)
            for k in range(TOPK):
                gather_v(UNITS - 1, (UNITS - 1) % 3, k)


def kernel(x, norm1_w, w_in, w_ret_o, w_pool_lin, pool_scale, w_pool_o, w_out, norm2_w, peer_w_q,
           peer_sub_keys, peer_u, peer_v, final_norm_w):
    import concourse.bacc as bacc
    from concourse.bass_utils import run_bass_kernel_spmd

    host = {
        "x": x[0], "norm1_w": norm1_w[0], "w_in": w_in[0], "w_ret_o": w_ret_o[0], "w_pool_lin": w_pool_lin[0],
        "pool_scale": np.asarray(pool_scale)[0].reshape(POOL_KC, P).T,
        "w_pool_o": w_pool_o[0], "w_out": w_out[0], "norm2_w": norm2_w[0], "peer_w_q": peer_w_q[0],
        "peer_sub_keys": np.asarray(peer_sub_keys)[0].transpose(2, 0, 1).reshape(P, 2 * NKEYS),
        "peer_u": peer_u[0], "peer_v": peer_v[0], "final_norm_w": final_norm_w,
    }
    host.update(constants())
    nc = bacc.Bacc("TRN2", target_bir_lowering=False, num_devices=1)
    arrays, aps = {}, {}
    for name, value in host.items():
        value = np.ascontiguousarray(value)
        arrays[f"in_{name}"] = value
        aps[name] = nc.dram_tensor(f"in_{name}", value.shape, mybir.dt.from_np(value.dtype), kind="ExternalInput").ap()
    out = nc.dram_tensor("out_dram", (SEQ, D), F32, kind="ExternalOutput").ap()
    build(nc, aps, out)
    r = run_bass_kernel_spmd(nc, [arrays], core_ids=[0])
    return r.results[0]["out_dram"].reshape(1, SEQ, D)
```

```python
from contextlib import ExitStack

import numpy as np

import concourse.bass as bass
from concourse import mybir

F32 = mybir.dt.float32
F32R = mybir.dt.float32r
U32 = mybir.dt.uint32
ALU = mybir.AluOpType
ACT = mybir.ActivationFunctionType
AX_X = mybir.AxisListType.X

P = 128
D = 2048
SEQ = 256
NB = SEQ // P
KC = D // P
HEADS, DK, DV = 8, 128, 256
Q_DIM, V_DIM = HEADS * DK, HEADS * DV
POOL_WINDOWS = (2, 4, 8, 16)
POOL_GROUPS, POOL_DIM = len(POOL_WINDOWS), 1024
POOL_GDIM = POOL_DIM // POOL_GROUPS
POOL_KC = POOL_DIM // P
PEER_HEADS, NKEYS, TOPK = 8, 128, 16
EPS = 1e-6
ROPE_BASE = 10000.0
NEG = -3.0e38

SLAB = 1024
HALF = 512
BANKS = NB * (SLAB // HALF)

Q0, K0, V0 = 0, Q_DIM, 2 * Q_DIM
G0 = V0 + V_DIM
P0 = G0 + V_DIM
GATE0 = P0 + POOL_DIM
MIX_COLS = GATE0
MIX_SLABS = MIX_COLS // SLAB
GATE_SLABS = 2 * D // SLAB
D_SLABS = D // SLAB
S_MIX = 0
S_GATE = S_MIX + MIX_SLABS
S_RET = S_GATE + GATE_SLABS
S_POOL = S_RET + D_SLABS
S_OUT = S_POOL + D_SLABS
S_Q = S_OUT + D_SLABS
S_END = S_Q + D_SLABS


def first_tile(slab):
    short = min(max(slab - S_POOL, 0), D_SLABS)
    return slab * KC - short * (KC - POOL_KC)


TILES = first_tile(S_END)
W_RING = 4
U_RING = 4
V_RING = 4
E_RING = 4
PICK_RING = 4
UNITS = NB * PEER_HEADS
HEADS_PER_SLAB = SLAB // (2 * NKEYS)



def constants():
    half = DK // 2
    inv_freq = (ROPE_BASE ** (-np.arange(half, dtype=np.float32) / half)).astype(np.float32)
    ang = np.arange(SEQ, dtype=np.float32)[:, None] * inv_freq[None, :]
    rope = np.stack([np.cos(ang), np.sin(ang)], 1).astype(np.float32)
    log_g = np.log(1.0 - 2.0 ** (-5.0 - np.arange(HEADS, dtype=np.float64)))
    diff = np.arange(SEQ)[None, :] - np.arange(P)[:, None]
    decay = np.where(diff[:, None] >= 0, np.exp(log_g[None, :, None] * np.maximum(diff, 0)[:, None]), 0.0)
    decay = decay * DK ** -0.5
    mask = decay.astype(np.float32)
    band = np.zeros((NB, P, POOL_GROUPS, SEQ), np.float32)
    for g, w in enumerate(POOL_WINDOWS):
        for t in range(SEQ):
            lo = max(0, t - w + 1)
            for s in range(lo, t + 1):
                band[s // P, s % P, g, t] = 1.0 / (t + 1 - lo) - (1.0 if s == t else 0.0)
    band = np.ascontiguousarray(band.transpose(1, 2, 0, 3))
    return {
        "rope": rope,
        "mask": mask.reshape(P, -1),
        "band": band.reshape(P, -1),
        "ident": np.eye(P, dtype=np.float32),
        "iota": np.tile(np.arange(NKEYS, dtype=np.float32), (P, 1)),
    }


def build(nc, a, out):
    with ExitStack() as ctx:
        def sb(name, shape, dt=F32):
            return ctx.enter_context(nc.sbuf_tensor(name, shape, dt))

        def sem(name):
            return ctx.enter_context(nc.semaphore(name))

        x_sb = sb("x_sb", [P, NB, D])
        rope_gate = sb("rope_gate", [P, 256])
        ident = sb("ident_sb", [P, P])
        iota = sb("iota_sb", [P, NKEYS])
        zeros = sb("zeros", [P, P])
        pscale = sb("pscale_sb", [P, POOL_KC])
        final_w = sb("final_w", [P, D])
        keys_hi = sb("keys_hi", [P, 2, NKEYS], F32R)
        keys_lo = sb("keys_lo", [P, 2, NKEYS], F32R)
        qk_tmp = sb("qk_tmp", [P, 1024])
        probs_picks = sb("probs_picks", [P, 1024])
        stat = sb("stat", [P, 2 * HEADS, 6])
        mean_var = sb("mean_var", [P, 2 * HEADS, 2])
        norm_a = sb("norm_a", [P, 2 * HEADS])
        norm_b = sb("norm_b", [P, 2 * HEADS])
        norm_c = sb("norm_c", [P, 2 * HEADS])
        top_val = sb("top_val", [P, 2, TOPK])
        top_idx = sb("top_idx", [P, 2, TOPK], U32)
        best = sb("best", [P, TOPK])
        best_pos = sb("best_pos", [P, TOPK], U32)
        pos_ab = sb("pos_ab", [P, 2, TOPK], U32)
        expert_ab = sb("expert_ab", [P, 2, TOPK])
        expert = sb("expert", [P, UNITS, TOPK], U32)
        weight = sb("weight", [P, UNITS, TOPK])
        idx_u = sb("idx_u", [P, 2, TOPK], U32)
        idx_v = sb("idx_v", [P, 2, TOPK], U32)
        dots = sb("dots", [P, TOPK])
        gelu = sb("gelu", [P, TOPK])
        gate_sum = sb("gate_sum", [P, 2])
        expert_f = sb("expert_f", [P, P])
        pick_int = sb("pick_int", [P, 3, P], U32)
        pick = sb("pick", [P, 3, P])
        pick_now = sb("pick_now", [P, 3, TOPK])

        rope = rope_gate[:, :].rearrange("p (t c f) -> p t c f", t=NB, c=2)
        gate = rope_gate[:, :].rearrange("p (u k) -> p u k", u=UNITS)
        keys_raw = expert[:, :, :].bitcast(F32).rearrange("p u k -> p (u k)").rearrange("p (h k) -> p h k", h=2)
        qk_t = qk_tmp[:, :].rearrange("p (r n t) -> p r n t", r=2, n=4)
        tmp_a, tmp_b = qk_tmp[:, 0:512], qk_tmp[:, 512:768]
        key_score = qk_tmp[:, 768:1024]
        staged = qk_tmp[:, :].rearrange("p (r b t) -> p r b t", r=4, b=NB)
        probs = probs_picks[:, 0:768].rearrange("p (r t) -> p r t", r=2)
        onehot = probs_picks[:, :].rearrange("p (r c k) -> p r c k", r=PICK_RING, c=2)

        with ExitStack() as lay:
            def first(name, shape, dt=F32):
                return lay.enter_context(nc.sbuf_tensor(name, shape, dt))

            act_hi = first("act_hi", [P, KC, SEQ], F32R)
            act_lo = first("act_lo", [P, KC, SEQ], F32R)
            pact_hi = first("pact_hi", [P, POOL_KC, SEQ], F32R)
            pact_lo = first("pact_lo", [P, POOL_KC, SEQ], F32R)
            w_hi = first("w_hi", [P, W_RING, SLAB], F32R)
            w_lo = first("w_lo", [P, W_RING, SLAB], F32R)
            w_raw = first("w_raw", [P, W_RING, SLAB])
            rows = first("rows", [P, NB, MIX_COLS])
            w_lin = first("w_lin", [P, POOL_GROUPS, 2, POOL_GDIM])
        with ExitStack() as lay:
            lay.enter_context(nc.sbuf_tensor("under_tables", [P, 2 * KC * SEQ], F32))
            mask = lay.enter_context(nc.sbuf_tensor("mask_sb", [P, HEADS, SEQ], F32))
            band = lay.enter_context(nc.sbuf_tensor("band_sb", [P, POOL_GROUPS, NB, SEQ], F32))
        with ExitStack() as lay:
            lay.enter_context(nc.sbuf_tensor("under_u_ring", [P, 6 * KC * SEQ], F32))
            u_ring = lay.enter_context(nc.sbuf_tensor("u_ring", [P, U_RING, D], F32))
        spread = [sb(f"spread{b}", [P, NKEYS, P]) for b in range(NB)]
        h2 = sb("h2", [P, NB, D])
        v_room = sb("v_room", [P, V_RING, D // 2])
        e_ring = h2[:, :, :].rearrange("p b (r c) -> p (b r) c", r=2)
        v_ring = v_room[:, :, :]
        h_rows = rows[:, :, 0:D]
        norm1 = rows[:, 0, D:2 * D]
        norm2 = v_room[:, 2:4, :].rearrange("p r c -> p (r c)")
        junk = v_room[:, 0:2, :].rearrange("p r c -> p (r c)")
        q_rows = v_room[:, 0:2, :]
        pooled = rows[:, 0, 0:2 * SLAB].rearrange("p (k t) -> p k t", k=POOL_KC)
        rope_tmp = rows[:, 0, G0:G0 + 2 * SLAB]

        bank = ctx.enter_context(nc.psum_tensor("bank", [P, BANKS, HALF], F32))
        misc = ctx.enter_context(nc.psum_tensor("misc", [P, 4, HALF], F32))
        scores_all = misc[:, :, :].rearrange("p b c -> p (b c)")

        x_landed = sem("x_landed")
        norm1_landed = sem("norm1_landed")
        const_landed = sem("const_landed")
        norm2_landed = sem("norm2_landed")
        final_landed = sem("final_landed")
        tile_landed = [sem(f"tile_landed{s}") for s in range(W_RING)]
        tile_hi = sem("tile_hi")
        tile_lo = sem("tile_lo")
        split_free = sem("split_free")
        bank_full = sem("bank_full")
        bank_free = sem("bank_free")
        squares_done = sem("squares_done")
        norm_step = sem("norm_step")
        root_done = sem("root_done")
        rows_ready = sem("rows_ready")
        turned = sem("turned")
        turned_hi = sem("turned_hi")
        turned_lo = sem("turned_lo")
        rope_done = sem("rope_done")
        qk_turned = sem("qk_turned")
        qk_copied = sem("qk_copied")
        scores_full = sem("scores_full")
        probs_ready = sem("probs_ready")
        y_full = sem("y_full")
        y_copied = sem("y_copied")
        pooled_full = sem("pooled_full")
        pooled_copied = sem("pooled_copied")
        lin_full = sem("lin_full")
        lin_hi = sem("lin_hi")
        lin_lo = sem("lin_lo")
        silu_done = sem("silu_done")
        y_normed = sem("y_normed")
        ret_ready = sem("ret_ready")
        pool_gated = sem("pool_gated")
        mixed_ready = sem("mixed_ready")
        resid_ready = sem("resid_ready")
        keys_hi_done = sem("keys_hi_done")
        keys_split = sem("keys_split")
        q_turned = sem("q_turned")
        q_hi = sem("q_hi")
        q_lo = sem("q_lo")
        key_scores = sem("key_scores")
        topk_done = sem("topk_done")
        exp_done = sem("exp_done")
        u_landed = [sem(f"u_landed{s}") for s in range(U_RING)]
        v_landed = [sem(f"v_landed{s}") for s in range(V_RING)]
        e_landed = [sem(f"e_landed{s}") for s in range(E_RING)]
        u_free = sem("u_free")
        v_free = sem("v_free")
        e_free = sem("e_free")
        gelu_ready = sem("gelu_ready")
        block_weighted = sem("block_weighted")
        picks_turned = sem("picks_turned")
        picks_ready = sem("picks_ready")
        onehot_ready = sem("onehot_ready")
        onehot_free = sem("onehot_free")
        spread_copied = sem("spread_copied")
        staged_ready = sem("staged_ready")
        y_peer_full = sem("y_peer_full")
        zeros_ready = sem("zeros_ready")
        dve_step = sem("dve_step")
        act_step = sem("act_step")
        pool_step = sem("pool_step")
        final_ready = sem("final_ready")
        pick_copied = sem("pick_copied")
        idx_doubled = sem("idx_doubled")
        dve_passed = sem("dve_passed")
        pool_passed = sem("pool_passed")
        stored = sem("stored")

        AHEAD = TOPK

        const_loads = [
            (keys_raw, a["peer_sub_keys"].rearrange("d (p k) -> d p k", p=2)),
            (rope, a["rope"].rearrange("(t p) c f -> p t c f", p=P)),
            (iota[:, :], a["iota"]),
            (final_w[:, :], a["final_norm_w"].rearrange("(o d) -> o d", o=1).to_broadcast([P, D])),
            (pscale[:, :], a["pool_scale"]),
            (mask[:, :, :], a["mask"].rearrange("p (h t) -> p h t", h=HEADS)),
            (band[:, :, :, :], a["band"].rearrange("p (g s t) -> p g s t", g=POOL_GROUPS, s=NB)),
            (w_lin[:, :, :, :], a["w_pool_lin"].rearrange("g (c p) d -> p g c d", p=P)),
        ]
        CONSTS = 16 * len(const_loads)

        class Steps:

            def __init__(self, eng, semaphore, base=0, apart=None):
                self.eng, self.sem, self.base, self.n, self.apart = eng, semaphore, base, 0, apart

            def __call__(self, ins):
                self.n += 1
                ins.then_inc(self.sem, 1)
                self.eng.wait_ge(self.sem, self.base + self.n)
                if self.apart is not None:
                    self.eng.sem_inc(self.apart, 1)

        block = ctx.enter_context(nc.Block())

        @block.sync
        def _(sp):
            sp.dma_start(x_sb[:, :, :], a["x"].rearrange("(t p) d -> p t d", p=P)).then_inc(x_landed, 16)
            sp.dma_start(norm1, a["norm1_w"].rearrange("(o d) -> o d", o=1).to_broadcast([P, D])).then_inc(norm1_landed, 16)

            def slab_tiles(w, col, t0, kc):
                for k in range(kc):
                    if not (isinstance(t0, int) and t0 + k < W_RING):
                        sp.wait_ge(tile_lo, t0 + (k + 1 - W_RING))
                    sp.dma_start(w_raw[:, k % W_RING, :], w[k * P:(k + 1) * P, bass.ds(col, SLAB)])\
                        .then_inc(tile_landed[k % W_RING], 16)

            sp.dma_start(ident[:, :], a["ident"]).then_inc(x_landed, 16)
            slab_tiles(a["w_in"], 0, 0, KC)
            for dst, src in const_loads:
                sp.dma_start(dst, src).then_inc(const_landed, 16)
            with sp.Fori(1, MIX_SLABS + GATE_SLABS) as j:
                slab_tiles(a["w_in"], j * SLAB, j * KC, KC)
            with sp.Fori(0, D_SLABS) as j:
                slab_tiles(a["w_ret_o"], j * SLAB, first_tile(S_RET) + j * KC, KC)
            sp.wait_ge(lin_full, POOL_GROUPS)
            sp.dma_start(norm2, a["norm2_w"].rearrange("(o d) -> o d", o=1).to_broadcast([P, D])).then_inc(norm2_landed, 16)
            with sp.Fori(0, D_SLABS) as j:
                slab_tiles(a["w_pool_o"], j * SLAB, first_tile(S_POOL) + j * POOL_KC, POOL_KC)
            with sp.Fori(0, D_SLABS) as j:
                slab_tiles(a["w_out"], j * SLAB, first_tile(S_OUT) + j * KC, KC)
            with sp.Fori(0, D_SLABS) as j:
                slab_tiles(a["peer_w_q"], j * SLAB, first_tile(S_Q) + j * KC, KC)
            lower = a["peer_v"].rearrange("(i j) d -> j i d", j=NKEYS)
            sp.wait_ge(u_free, AHEAD + U_RING + UNITS * TOPK)
            with sp.Fori(0, NKEYS // E_RING) as i:
                for r in range(E_RING):
                    sp.wait_ge(e_free, i * E_RING + r + 1)
                    sp.dma_start(e_ring[:, r, :], lower[bass.ds(i * E_RING + r, 1), :, 0:D // 2].rearrange("o i d -> i (o d)"))\
                        .then_inc(e_landed[r], 16)
            for b in range(NB):
                sp.wait_ge(final_ready, b + 1)
                sp.dma_start(out[b * P:(b + 1) * P, :], h2[:, b, :]).then_inc(stored, 16)
            sp.wait_ge(stored, 16 * NB)

        @block.tensor
        def _(pe):
            pe.sem_inc(split_free, W_RING)
            pe.sem_inc(e_free, E_RING)
            pe.sem_inc(onehot_free, PICK_RING)

            def slab(s, t0, kc, hi, lo):
                for k in range(kc):
                    r = k % W_RING
                    pe.wait_ge(tile_lo, t0 + k + 1)
                    for t in range(NB):
                        for h in range(2):
                            b = 2 * t + h
                            if k == 0:
                                pe.wait_ge(bank_free, 4 * s + b + 1)
                            o = bank[:, b, :]
                            rh, rl = w_hi[:, r, h * HALF:(h + 1) * HALF], w_lo[:, r, h * HALF:(h + 1) * HALF]
                            lh, ll = hi[:, k, t * P:(t + 1) * P], lo[:, k, t * P:(t + 1) * P]
                            pe.matmul(o, lh, rh, start=(k == 0), stop=False)
                            pe.matmul(o, lh, rl, start=False, stop=False)
                            m = pe.matmul(o, ll, rh, start=False, stop=(k == kc - 1))
                            if k == kc - 1:
                                m.then_inc(bank_full, 1)
                    (pe.drain() if k == kc - 1 else m).then_inc(split_free, 1)

            def turn(stage, src, ready):
                for f in range(8):
                    j, t, h = f // 4, (f // 2) % 2, f % 2
                    for s, n in ready(f):
                        pe.wait_ge(s, n)
                    if stage or f >= 4:
                        pe.wait_ge(turned_lo, 8 * stage + f - 3)
                    for c in range(4):
                        col = j * SLAB + h * HALF + c * P
                        m = pe.transpose(misc[:, f % 4, c * P:(c + 1) * P], src[:, t, col:col + P], ident[:, :])
                    m.then_inc(turned, 1)

            pe.wait_ge(x_landed, 32)
            turn(0, h_rows, lambda f: [(rows_ready, (f // 2) % 2 + 1)])
            pe.wait_ge(turned_lo, 8)
            with pe.Fori(0, MIX_SLABS) as j:
                slab(j, j * KC, KC, act_hi, act_lo)

            pe.wait_ge(rope_done, 2 * NB)
            for i in range(HEADS + 2):
                if i < HEADS:
                    h = i
                    if h >= 2:
                        pe.wait_ge(qk_copied, h - 1)
                    for n in range(4):
                        col = (Q0 if n < 2 else K0) + h * DK
                        m = pe.transpose(misc[:, h % 2, n * P:(n + 1) * P], rows[:, n % 2, col:col + DK], ident[:, :])
                    m.then_inc(qk_turned, 1)
                if 1 <= i <= HEADS:
                    h = i - 1
                    pe.wait_ge(qk_copied, h + 1)
                    if h >= 1:
                        pe.wait_ge(probs_ready, h)
                    q = qk_t[:, h % 2, 0:2, :].rearrange("p n t -> p (n t)")
                    pe.matmul(misc[:, 2, 0:2 * P], qk_t[:, h % 2, 2, :], q, start=True, stop=True)
                    pe.matmul(misc[:, 2, 2 * P:3 * P], qk_t[:, h % 2, 3, :], qk_t[:, h % 2, 1, :],
                              start=True, stop=True).then_inc(scores_full, 1)
                if i >= 2:
                    h = i - 2
                    pe.wait_ge(probs_ready, h + 1)
                    if h == 0:
                        pe.wait_ge(bank_free, 4 * MIX_SLABS)
                    else:
                        pe.wait_ge(y_copied, h)
                    v = [rows[:, t, V0 + h * DV:V0 + (h + 1) * DV] for t in range(NB)]
                    pr = probs[:, h % 2, :]
                    pe.matmul(misc[:, 3, 0:DV], pr[:, 0:P], v[0], start=True, stop=True)
                    pe.matmul(misc[:, 3, DV:2 * DV], pr[:, P:2 * P], v[0], start=True, stop=False)
                    pe.matmul(misc[:, 3, DV:2 * DV], pr[:, 2 * P:3 * P], v[1], start=False, stop=True)\
                        .then_inc(y_full, 1)

            pe.wait_ge(const_landed, CONSTS)
            pe.wait_ge(bank_free, 4 * MIX_SLABS + 4)
            pe.wait_ge(y_copied, HEADS)
            for f in range(POOL_GROUPS):
                for c in range(2):
                    col = P0 + (2 * f + c) * P
                    o = misc[:, f, c * SEQ:(c + 1) * SEQ]
                    pe.matmul(o, rows[:, 0, col:col + P], band[:, f, 0, :], start=True, stop=False)
                    m = pe.matmul(o, rows[:, 1, col:col + P], band[:, f, 1, :], start=False, stop=True)
                m.then_inc(pooled_full, 1)
            for f in range(POOL_GROUPS):
                pe.wait_ge(pooled_copied, f + 1)
                for d in range(2):
                    o = misc[:, f, d * SEQ:(d + 1) * SEQ]
                    for c in range(2):
                        m = pe.matmul(o, w_lin[:, f, c, d * P:(d + 1) * P], pooled[:, 2 * f + c, :],
                                      start=(c == 0), stop=(c == 1))
                m.then_inc(lin_full, 1)

            with pe.Fori(S_GATE, S_RET) as j:
                slab(j, j * KC, KC, act_hi, act_lo)

            pe.wait_ge(lin_lo, POOL_GROUPS)
            turn(1, rows[:, :, G0:G0 + D], lambda f: [(ret_ready, (f // 2) % 2 + 1)])
            pe.wait_ge(turned_lo, 16)
            with pe.Fori(0, D_SLABS) as j:
                slab(S_RET + j, first_tile(S_RET) + j * KC, KC, act_hi, act_lo)
            with pe.Fori(0, D_SLABS) as j:
                slab(S_POOL + j, first_tile(S_POOL) + j * POOL_KC, POOL_KC, pact_hi, pact_lo)

            turn(2, rows[:, :, 0:D], lambda f: [(mixed_ready, f + 1)])
            pe.wait_ge(turned_lo, 24)
            with pe.Fori(0, D_SLABS) as j:
                slab(S_OUT + j, first_tile(S_OUT) + j * KC, KC, act_hi, act_lo)

            turn(3, h2, lambda f: [(rows_ready, 2 + (f // 2) % 2 + 1)])
            pe.wait_ge(turned_lo, 32)
            pe.wait_ge(keys_split, 1)
            for j in range(D_SLABS):
                slab(S_Q + j, first_tile(S_Q + j), KC, act_hi, act_lo)
                if j:
                    pe.wait_ge(topk_done, 2 * HEADS_PER_SLAB * j)
                for f in range(4):
                    t, g = f // 2, f % 2
                    pe.wait_ge(bank_free, 4 * (S_Q + j) + BANKS + f + 1)
                    for c in range(4):
                        m = pe.transpose(misc[:, f, c * P:(c + 1) * P],
                                         q_rows[:, t, (4 * g + c) * P:(4 * g + c + 1) * P], ident[:, :])
                    m.then_inc(q_turned, 1)
                pe.wait_ge(q_lo, 4 * (j + 1))
                for t in range(NB):
                    for c in range(8):
                        o = misc[:, 2 * t + c // 4, (c % 4) * P:(c % 4 + 1) * P]
                        lh, ll = pact_hi[:, c, t * P:(t + 1) * P], pact_lo[:, c, t * P:(t + 1) * P]
                        rh, rl = keys_hi[:, c % 2, :], keys_lo[:, c % 2, :]
                        pe.matmul(o, lh, rh, start=True, stop=False)
                        pe.matmul(o, lh, rl, start=False, stop=False)
                        m = pe.matmul(o, ll, rh, start=False, stop=True)
                    m.then_inc(key_scores, 1)

            pe.wait_ge(topk_done, UNITS)
            for b in range(NB):
                pe.wait_ge(block_weighted, b + 1)
                pe.transpose(bank[:, 0, 0:P], expert_f[:, :], ident[:, :])
                pe.transpose(bank[:, 0, P:2 * P], weight[:, b * PEER_HEADS:(b + 1) * PEER_HEADS, :].rearrange("p u k -> p (u k)"),
                             ident[:, :]).then_inc(picks_turned, 1)
                with pe.Fori(b * PEER_HEADS, (b + 1) * PEER_HEADS) as i:
                    for n in range(TOPK):
                        pe.wait_ge(onehot_ready, i * TOPK + n + 1)
                        if n % 4 == 0:
                            pe.wait_ge(spread_copied, i * 4 + n // 4 + 1)
                        m = pe.matmul(misc[:, n // 4, (n % 4) * P:(n % 4 + 1) * P], onehot[:, n % PICK_RING, 0, :],
                                      onehot[:, n % PICK_RING, 1, :], start=True, stop=True)
                        m.then_inc(onehot_free, 1)

            pe.wait_ge(zeros_ready, 1)
            pe.wait_ge(picks_ready, NB)
            blank = zeros[:, :].unsqueeze(1).to_broadcast([P, HALF // P, P])
            for n in range(BANKS):
                pe.matmul(bank[:, n, :], zeros[:, :], blank, start=True, stop=False, skip_group_check=True)
            with pe.Fori(0, NKEYS // E_RING) as i:
                for r in range(E_RING):
                    pe.wait_ge(staged_ready, i * E_RING + r + 1)
                    pe.wait_ge(e_landed[r], i * 16 + 16)
                    for b in range(NB):
                        for h in range(2):
                            m = pe.matmul(bank[:, 2 * b + h, :], staged[:, r, b, :], e_ring[:, r, h * HALF:(h + 1) * HALF],
                                          start=False, stop=False, skip_group_check=True)
                    m.then_inc(e_free, 1)
            for n in range(BANKS):
                m = pe.matmul(bank[:, n, :], zeros[:, :], blank, start=False, stop=True, skip_group_check=True)
            m.then_inc(y_peer_full, 1)

        @block.scalar
        def _(act):
            act.sem_inc(bank_free, BANKS)
            act.sem_inc(spread_copied, 4)
            step = Steps(act, act_step)

            def tiles(t0, n):
                for k in range(n):
                    r = k % W_RING
                    act.wait_ge(split_free, t0 + k + 1)
                    act.wait_ge(tile_landed[r], landed(t0, k))
                    act.activation(w_hi[:, r, :], w_raw[:, r, :], ACT.Copy).then_inc(tile_hi, 1)

            def landed(t0, k):
                return t0 * (16 // W_RING) + 16 * (k // W_RING + 1)

            def turned_high(stage):
                for f in range(8):
                    n = 8 * stage + f + 1
                    j, t, h = f // 4, (f // 2) % 2, f % 2
                    c = (j * SLAB + h * HALF) // P
                    act.wait_ge(turned, n)
                    act.activation(act_hi[:, c:c + 4, t * P:(t + 1) * P],
                                   misc[:, f % 4, :].rearrange("p (c t) -> p c t", c=4), ACT.Copy).then_inc(turned_hi, 1)

            def squares(n0):
                for t in range(NB):
                    step(act.activation(junk, x_sb[:, t, :], ACT.Square, accum_out=norm_a[:, t:t + 1]))
                act.sem_inc(squares_done, 1)
                act.wait_ge(norm_step, n0)
                act.activation(norm_c[:, 0:NB], norm_b[:, 0:NB], ACT.Sqrt).then_inc(root_done, 1)

            act.wait_ge(x_landed, 32)
            squares(1)
            tiles(0, W_RING)
            turned_high(0)
            for first, last in ((0, G0 // SLAB), (G0 // SLAB, MIX_SLABS)):
                if first:
                    act.wait_ge(rope_done, 2 * NB)
                with act.Fori(first, last) as j:
                    tiles(j * KC + W_RING, KC)
                    for b in range(BANKS):
                        act.wait_ge(bank_full, 4 * j + b + 1)
                        act.activation(rows[:, b // 2, bass.ds(j * SLAB + (b % 2) * HALF, HALF)], bank[:, b, :], ACT.Copy)\
                            .then_inc(bank_free, 1)
            for i in range(HEADS + 2):
                if i < HEADS:
                    act.wait_ge(qk_turned, i + 1)
                    if i >= 2:
                        act.wait_ge(scores_full, i - 1)
                    act.activation(qk_t[:, i % 2, :, :].rearrange("p n t -> p (n t)"), misc[:, i % 2, :], ACT.Copy)\
                        .then_inc(qk_copied, 1)
                if i >= 2:
                    h = i - 2
                    act.wait_ge(y_full, h + 1)
                    act.activation(rows[:, :, V0 + h * DV:V0 + (h + 1) * DV],
                                   misc[:, 3, :].rearrange("p (t c) -> p t c", t=NB), ACT.Copy).then_inc(y_copied, 1)
            for f in range(POOL_GROUPS):
                act.wait_ge(pooled_full, f + 1)
                act.activation(pooled[:, 2 * f:2 * f + 2, :].rearrange("p k t -> p (k t)"), misc[:, f, :], ACT.Copy)\
                    .then_inc(pooled_copied, 1)
            for f in range(POOL_GROUPS):
                act.wait_ge(lin_full, f + 1)
                for d in range(2):
                    m = act.activation(pact_hi[:, 2 * f + d, :], misc[:, f, d * SEQ:(d + 1) * SEQ], ACT.Copy,
                                       scale=pscale[:, 2 * f + d:2 * f + d + 1])
                m.then_inc(lin_hi, 1)
            for t in range(NB):
                act.activation(rows[:, t, G0:G0 + V_DIM], rows[:, t, G0:G0 + V_DIM], ACT.Silu).then_inc(silu_done, 1)
            act.wait_ge(norm_step, 2)
            act.activation(norm_c[:, :], norm_b[:, :], ACT.Sqrt).then_inc(root_done, 1)
            act.activation(keys_hi[:, :, :], keys_raw, ACT.Copy).then_inc(keys_hi_done, 1)
            for first, last in ((0, V0 // SLAB), (V0 // SLAB, GATE_SLABS)):
                if first:
                    act.wait_ge(ret_ready, NB)
                with act.Fori(first, last) as j:
                    tiles(j * KC + first_tile(S_GATE) + W_RING, KC)
                    for b in range(BANKS):
                        act.wait_ge(bank_full, 4 * j + (4 * S_GATE + b + 1))
                        act.activation(rows[:, b // 2, bass.ds(j * SLAB + (b % 2) * HALF, HALF)], bank[:, b, :],
                                       ACT.Sigmoid).then_inc(bank_free, 1)
            turned_high(1)
            with act.Fori(0, D_SLABS) as j:
                tiles(j * KC + first_tile(S_RET) + W_RING, KC)
            with act.Fori(0, D_SLABS) as j:
                tiles(j * POOL_KC + first_tile(S_POOL) + W_RING, POOL_KC)
            turned_high(2)
            with act.Fori(0, D_SLABS) as j:
                tiles(j * KC + first_tile(S_OUT) + W_RING, KC)
            act.wait_ge(bank_free, 4 * S_Q + BANKS)
            squares(3)
            turned_high(3)

            def q_copy(j):
                for b in range(BANKS):
                    act.wait_ge(bank_full, 4 * (S_Q + j) + b + 1)
                    act.activation(q_rows[:, b // 2, (b % 2) * HALF:(b % 2 + 1) * HALF], bank[:, b, :], ACT.Copy)\
                        .then_inc(bank_free, 1)
                for f in range(4):
                    t, g = f // 2, f % 2
                    act.wait_ge(q_turned, 4 * j + f + 1)
                    act.activation(pact_hi[:, 4 * g:4 * g + 4, t * P:(t + 1) * P],
                                   misc[:, f, :].rearrange("p (c t) -> p c t", c=4), ACT.Copy).then_inc(q_hi, 1)

            def numerators(u0, n):
                act.activation(gate[:, bass.ds(u0, n), :], gate[:, bass.ds(u0, n), :], ACT.Exp).then_inc(exp_done, n)

            def gelu_unit(u):
                act.wait_ge(u_free, u * TOPK + (AHEAD + U_RING + TOPK))
                act.activation(gelu[:, :], dots[:, :], ACT.Gelu).then_inc(gelu_ready, 1)

            def spread_out(b, i, n):
                act.wait_ge(onehot_free, i * TOPK + (4 * n + 4 + PICK_RING))
                t0 = i * TOPK + (4 * n - b * P)
                act.activation(spread[b][:, :, bass.ds(t0, 4)], misc[:, n, :].rearrange("p (t k) -> p k t", t=4), ACT.Copy)\
                    .then_inc(spread_copied, 1)

            tiles(first_tile(S_Q) + W_RING, KC)
            q_copy(0)
            act.wait_ge(topk_done, 4)
            numerators(0, 4)
            tiles(first_tile(S_Q + 1) + W_RING, W_RING)
            gelu_unit(0)
            act.wait_ge(topk_done, 8)
            numerators(PEER_HEADS, 4)
            tiles(first_tile(S_Q + 1) + 2 * W_RING, 2 * W_RING)
            gelu_unit(1)
            q_copy(1)
            gelu_unit(2)
            act.wait_ge(topk_done, 12)
            numerators(4, 4)
            for u in range(3, 6):
                gelu_unit(u)
            act.wait_ge(topk_done, UNITS)
            numerators(PEER_HEADS + 4, 4)
            for u in range(6, 8):
                gelu_unit(u)
            with act.Fori(PEER_HEADS, UNITS) as u:
                for n in range(4):
                    spread_out(0, u - PEER_HEADS, n)
                gelu_unit(u)
            with act.Fori(PEER_HEADS, UNITS) as i:
                for n in range(4):
                    spread_out(1, i, n)
            act.wait_ge(spread_copied, 4 + SEQ // 4)
            with act.Fori(0, NKEYS // E_RING) as i:
                for r in range(E_RING):
                    act.wait_ge(e_free, i * E_RING + r + 1)
                    for b in range(NB):
                        m = act.activation(staged[:, r, b, :], spread[b][:, bass.ds(i * E_RING + r, 1), :]
                                           .rearrange("p o t -> p (o t)"), ACT.Copy)
                    m.then_inc(staged_ready, 1)
            for b in range(NB):
                act.wait_ge(resid_ready, b + 1)
                step(act.activation(junk, x_sb[:, b, :], ACT.Square, accum_out=norm_a[:, b:b + 1]))
                act.sem_inc(squares_done, 1)
            act.wait_ge(norm_step, 4)
            act.activation(norm_c[:, 0:NB], norm_b[:, 0:NB], ACT.Sqrt).then_inc(root_done, 1)

        @block.vector
        def _(dve):
            dve.sem_inc(u_free, AHEAD + U_RING)
            dve.sem_inc(v_free, AHEAD + V_RING)
            step = Steps(dve, dve_step)

            def tiles(t0, n):
                for k in range(n):
                    r = k % W_RING
                    dve.wait_ge(tile_hi, t0 + k + 1)
                    dve.tensor_tensor(w_lo[:, r, :], w_raw[:, r, :], w_hi[:, r, :].bitcast(F32), ALU.subtract)\
                        .then_inc(tile_lo, 1)

            def turned_low(stage):
                for f in range(8):
                    n = 8 * stage + f + 1
                    j, t, h = f // 4, (f // 2) % 2, f % 2
                    c = (j * SLAB + h * HALF) // P
                    dve.wait_ge(turned_hi, n)
                    dve.tensor_tensor(act_lo[:, c:c + 4, t * P:(t + 1) * P],
                                      misc[:, f % 4, :].rearrange("p (c t) -> p c t", c=4),
                                      act_hi[:, c:c + 4, t * P:(t + 1) * P].bitcast(F32), ALU.subtract)\
                        .then_inc(turned_lo, 1)

            def inverse_root(n, width):
                dve.sem_inc(norm_step, 1)
                dve.wait_ge(root_done, n)
                a_, b_, c_ = norm_a[:, 0:width], norm_b[:, 0:width], norm_c[:, 0:width]
                step(dve.reciprocal(a_, c_))
                step(dve.tensor_tensor(c_, a_, a_, ALU.mult))
                step(dve.tensor_tensor(c_, c_, b_, ALU.mult))
                step(dve.tensor_scalar(c_, c_, -0.5, 1.5, ALU.mult, ALU.add))
                step(dve.tensor_tensor(a_, a_, c_, ALU.mult))

            def norm_factor(n, n_squares):
                dve.wait_ge(squares_done, n_squares)
                step(dve.tensor_scalar(norm_b[:, 0:NB], norm_a[:, 0:NB], 1.0 / D, EPS, ALU.mult, ALU.add))
                inverse_root(n, NB)

            norm_factor(1, 1)
            dve.wait_ge(norm1_landed, 16)
            for t in range(NB):
                dve.scalar_tensor_tensor(h_rows[:, t, :], x_sb[:, t, :], norm_a[:, t:t + 1], norm1, ALU.mult, ALU.mult)\
                    .then_inc(rows_ready, 1)
            tiles(0, W_RING)
            turned_low(0)
            with dve.Fori(0, MIX_SLABS) as j:
                tiles(j * KC + W_RING, KC)
            dve.wait_ge(const_landed, CONSTS)
            for h in range(HEADS):
                dve.wait_ge(scores_full, h + 1)
                if h >= 2:
                    dve.wait_ge(y_full, h - 1)
                dve.tensor_tensor(probs[:, h % 2, 0:SEQ], misc[:, 2, 0:SEQ], mask[:, h, :], ALU.mult)
                dve.tensor_tensor(probs[:, h % 2, SEQ:SEQ + P], misc[:, 2, SEQ:SEQ + P], mask[:, h, 0:P], ALU.mult)\
                    .then_inc(probs_ready, 1)
            for f in range(POOL_GROUPS):
                dve.wait_ge(lin_hi, f + 1)
                for d in range(2):
                    c = 2 * f + d
                    m = dve.scalar_tensor_tensor(pact_lo[:, c, :], misc[:, f, d * SEQ:(d + 1) * SEQ], pscale[:, c:c + 1],
                                                 pact_hi[:, c, :].bitcast(F32), ALU.mult, ALU.subtract)
                m.then_inc(lin_lo, 1)
            dve.wait_ge(y_copied, HEADS)
            for n in range(2 * HEADS):
                t, h = n // HEADS, n % HEADS
                m = dve.bn_stats(stat[:, n, :], rows[:, t, V0 + h * DV:V0 + (h + 1) * DV])
            step(m)
            for n in range(2 * HEADS):
                m = dve.bn_aggr(mean_var[:, n, :], stat[:, n, :])
            step(m)
            step(dve.tensor_scalar(norm_b[:, :], mean_var[:, :, 1], EPS, None, ALU.add))
            inverse_root(2, 2 * HEADS)
            for t in range(NB):
                for h in range(HEADS):
                    y = rows[:, t, V0 + h * DV:V0 + (h + 1) * DV]
                    n = t * HEADS + h
                    m = dve.tensor_scalar(y, y, mean_var[:, n, 0:1], norm_a[:, n:n + 1], ALU.subtract, ALU.mult)
                m.then_inc(y_normed, 1)
            dve.memset(zeros[:, :], 0.0).then_inc(zeros_ready, 1)
            dve.wait_ge(keys_hi_done, 1)
            dve.tensor_tensor(keys_lo[:, :, :], keys_raw, keys_hi[:, :, :].bitcast(F32), ALU.subtract)\
                .then_inc(keys_split, 1)
            with dve.Fori(0, GATE_SLABS) as j:
                tiles(j * KC + first_tile(S_GATE) + W_RING, KC)
            turned_low(1)
            with dve.Fori(0, D_SLABS) as j:
                tiles(j * KC + first_tile(S_RET) + W_RING, KC)
                for b in range(BANKS):
                    dve.wait_ge(bank_full, 4 * j + (4 * S_RET + b + 1))
                    g = rows[:, b // 2, bass.ds(j * SLAB + (b % 2) * HALF, HALF)]
                    dve.tensor_tensor(g, g, bank[:, b, :], ALU.mult).then_inc(bank_free, 1)
            with dve.Fori(0, D_SLABS) as j:
                tiles(j * POOL_KC + first_tile(S_POOL) + W_RING, POOL_KC)
                for b in range(BANKS):
                    dve.wait_ge(bank_full, 4 * j + (4 * S_POOL + b + 1))
                    g = rows[:, b // 2, bass.ds(j * SLAB + (D + (b % 2) * HALF), HALF)]
                    dve.tensor_tensor(g, g, bank[:, b, :], ALU.mult).then_inc(bank_free, 1)
            turned_low(2)
            with dve.Fori(0, D_SLABS) as j:
                tiles(j * KC + first_tile(S_OUT) + W_RING, KC)
                for b in range(BANKS):
                    dve.wait_ge(bank_full, 4 * j + (4 * S_OUT + b + 1))
                    g = x_sb[:, b // 2, bass.ds(j * SLAB + (b % 2) * HALF, HALF)]
                    dve.tensor_tensor(g, g, bank[:, b, :], ALU.add).then_inc(bank_free, 1)
            norm_factor(3, 2)
            dve.wait_ge(norm2_landed, 16)
            dve.wait_ge(turned, 24)
            for t in range(NB):
                dve.scalar_tensor_tensor(h2[:, t, :], x_sb[:, t, :], norm_a[:, t:t + 1], norm2, ALU.mult, ALU.mult)\
                    .then_inc(rows_ready, 1)
            turned_low(3)

            def q_low(j):
                for f in range(4):
                    t, g = f // 2, f % 2
                    dve.wait_ge(q_hi, 4 * j + f + 1)
                    dve.tensor_tensor(pact_lo[:, 4 * g:4 * g + 4, t * P:(t + 1) * P],
                                      misc[:, f, :].rearrange("p (c t) -> p c t", c=4),
                                      pact_hi[:, 4 * g:4 * g + 4, t * P:(t + 1) * P].bitcast(F32), ALU.subtract)\
                        .then_inc(q_lo, 1)

            TOPK_STEPS = 16

            def two_rounds(st, pairs, work):
                for src, val, pos in pairs:
                    m = dve.max(val[:, 0:8], src)
                st(m)
                for src, val, pos in pairs:
                    dve.max_index(pos[:, 0:8], val[:, 0:8], src)
                for (src, val, pos), w in zip(pairs, work):
                    m = dve.match_replace(w, val[:, 0:8], src, NEG)
                st(m)
                for (src, val, pos), w in zip(pairs, work):
                    m = dve.max(val[:, 8:16], w)
                st(m)
                for (src, val, pos), w in zip(pairs, work):
                    m = dve.max_index(pos[:, 8:16], val[:, 8:16], w)
                st(m)

            def top_experts(n, u, base):
                st = Steps(dve, dve_step, base, dve_passed)
                s = key_score[:, :]
                st(dve.tensor_copy(s, scores_all[:, bass.ds(n * 2 * NKEYS, 2 * NKEYS)]))
                two_rounds(st, [(s[:, p * NKEYS:(p + 1) * NKEYS], top_val[:, p, :], top_idx[:, p, :]) for p in range(2)],
                           [tmp_a[:, p * NKEYS:(p + 1) * NKEYS] for p in range(2)])
                grid = [P, TOPK, TOPK]
                cand = tmp_b[:, 0:TOPK * TOPK]
                st(dve.tensor_tensor(cand.rearrange("p (a b) -> p a b", a=TOPK),
                                     top_val[:, 0, :].unsqueeze(2).to_broadcast(grid),
                                     top_val[:, 1, :].unsqueeze(1).to_broadcast(grid), ALU.add))
                two_rounds(st, [(cand, best[:, :], best_pos[:, :])], [tmp_a[:, 0:TOPK * TOPK]])
                st(dve.tensor_scalar(gate[:, bass.ds(u, 1), :].rearrange("p u k -> p (u k)"), best[:, :], best[:, 0:1], None,
                                     ALU.subtract))
                dve.tensor_single_scalar(pos_ab[:, 0, :], best_pos[:, :], 4, ALU.logical_shift_right)
                st(dve.tensor_single_scalar(pos_ab[:, 1, :], best_pos[:, :], TOPK - 1, ALU.bitwise_and))
                hits = tmp_a[:, :].rearrange("p (h k j) -> p h k j", h=2, k=TOPK)
                for p in range(2):
                    m = dve.tensor_tensor(hits[:, p, :, :], pos_ab[:, p, :].unsqueeze(2).to_broadcast(grid),
                                          iota[:, 0:TOPK].unsqueeze(1).to_broadcast(grid), ALU.is_equal)
                st(m)
                for p in range(2):
                    m = dve.tensor_tensor(hits[:, p, :, :], hits[:, p, :, :],
                                          top_idx[:, p, :].unsqueeze(1).to_broadcast(grid), ALU.mult)
                st(m)
                st(dve.tensor_reduce(expert_ab[:, :, :], hits, AX_X, ALU.add))
                st(dve.scalar_tensor_tensor(expert[:, bass.ds(u, 1), :].rearrange("p u k -> p (u k)"), expert_ab[:, 0, :],
                                            float(NKEYS), expert_ab[:, 1, :], ALU.mult, ALU.add))
                assert st.n <= TOPK_STEPS
                if st.n < TOPK_STEPS:
                    dve.sem_inc(dve_step, TOPK_STEPS - st.n)
                dve.sem_inc(topk_done, 1)

            def top_heads(j, b, h, n=2):
                before = step.n
                with dve.Fori(0, n) as i:
                    top_experts(i + (b * HEADS_PER_SLAB + h), i + (b * PEER_HEADS + j * HEADS_PER_SLAB + h),
                                i * TOPK_STEPS + before)
                step.n += n * TOPK_STEPS

            UNIT_STEPS = 3

            def dot_products(u0, n):
                before = step.n
                b = u0 // PEER_HEADS
                with dve.Fori(u0, u0 + n) as u:
                    st = Steps(dve, dve_step, (u - u0) * UNIT_STEPS + before)
                    for k in range(TOPK):
                        r = k % U_RING
                        dve.wait_ge(u_landed[r], u * (16 * TOPK // U_RING) + 16 * (k // U_RING + 1))
                        dve.tensor_tensor_reduce(out=u_ring[:, r, :], in0=u_ring[:, r, :], in1=h2[:, b, :], scale=1.0,
                                                 scalar=0.0, op0=ALU.mult, op1=ALU.add, accum_out=dots[:, k:k + 1])\
                            .then_inc(u_free, 1)
                    g = gate[:, bass.ds(u, 1), :].rearrange("p u k -> p (u k)")
                    dve.wait_ge(exp_done, 4 if u0 < 4 else 12 if u0 < 8 else 16)
                    st(dve.tensor_reduce(gate_sum[:, 0:1], g, AX_X, ALU.add))
                    st(dve.reciprocal(gate_sum[:, 1:2], gate_sum[:, 0:1]))
                    dve.wait_ge(gelu_ready, u + 1)
                    st(dve.scalar_tensor_tensor(weight[:, bass.ds(u, 1), :].rearrange("p u k -> p (u k)"), gelu[:, :],
                                                gate_sum[:, 1:2], g, ALU.mult, ALU.mult))
                step.n += n * UNIT_STEPS

            def turn_picks(b):
                step(dve.tensor_copy(expert_f[:, :], expert[:, b * PEER_HEADS:(b + 1) * PEER_HEADS, :].rearrange("p u k -> p (u k)")))
                dve.sem_inc(block_weighted, 1)
                dve.wait_ge(picks_turned, b + 1)
                if b:
                    dve.wait_ge(onehot_ready, P)
                dve.tensor_copy(pick[:, 2, :], bank[:, 0, P:2 * P])
                step(dve.tensor_copy(pick_int[:, 0, :], bank[:, 0, 0:P]))
                dve.tensor_single_scalar(pick_int[:, 1, :], pick_int[:, 0, :], 7, ALU.logical_shift_right)
                step(dve.tensor_single_scalar(pick_int[:, 2, :], pick_int[:, 0, :], NKEYS - 1, ALU.bitwise_and))
                step(dve.tensor_copy(pick[:, 0:2, :], pick_int[:, 1:3, :]))
                dve.sem_inc(picks_ready, 1)

            tiles(first_tile(S_Q) + W_RING, KC)
            q_low(0)
            dve.wait_ge(key_scores, 2)
            top_heads(0, 0, 0, 4)
            tiles(first_tile(S_Q + 1) + W_RING, W_RING)
            dot_products(0, 1)
            top_heads(0, 1, 0, 4)
            tiles(first_tile(S_Q + 1) + 2 * W_RING, 2 * W_RING)
            dot_products(1, 1)
            q_low(1)
            dve.wait_ge(key_scores, 4)
            dot_products(2, 1)
            top_heads(1, 0, 0, 4)
            dot_products(3, 1)
            top_heads(1, 1, 0)
            dot_products(4, 1)
            top_heads(1, 1, 2)
            dot_products(5, 3)
            turn_picks(0)
            dot_products(PEER_HEADS, PEER_HEADS)
            turn_picks(1)
            with dve.Fori(0, PEER_HEADS) as i:
                for n in range(TOPK):
                    dve.wait_ge(onehot_free, i * TOPK + (P + n + 1))
                    key = [pick[:, c, bass.ds(i * TOPK + n, 1)] for c in range(3)]
                    dve.tensor_scalar(onehot[:, n % PICK_RING, 0, :], iota[:, :], key[0], None, ALU.is_equal)
                    dve.tensor_scalar(onehot[:, n % PICK_RING, 1, :], iota[:, :], key[1], key[2], ALU.is_equal, ALU.mult)\
                        .then_inc(onehot_ready, 1)
            for b in range(NB):
                before = step.n
                with dve.Fori(b * PEER_HEADS, (b + 1) * PEER_HEADS) as u:
                    acc = x_sb[:, b, D // 2:D]
                    for k in range(TOPK):
                        r = k % V_RING
                        dve.wait_ge(v_landed[r], u * (16 * TOPK // V_RING) + 16 * (k // V_RING + 1))
                        dve.wait_ge(v_free, u * TOPK + (AHEAD + V_RING + k))
                        dve.scalar_tensor_tensor(acc, v_ring[:, r, :], weight[:, bass.ds(u, 1), k:k + 1].rearrange("p u k -> p (u k)"),
                                                 acc, ALU.mult, ALU.add).then_inc(v_free, 1)

            dve.wait_ge(y_peer_full, 1)
            dve.wait_ge(v_free, AHEAD + V_RING + UNITS * TOPK)
            for b in range(NB):
                step(dve.tensor_tensor(x_sb[:, b, 0:D // 2], x_sb[:, b, 0:D // 2],
                                       bank[:, 2 * b:2 * b + 2, :].rearrange("p b c -> p (b c)"), ALU.add))
                dve.sem_inc(resid_ready, 1)
            norm_factor(4, 4)
            for b in range(NB):
                dve.scalar_tensor_tensor(h2[:, b, :], x_sb[:, b, :], norm_a[:, b:b + 1], final_w[:, :], ALU.mult, ALU.mult)\
                    .then_inc(final_ready, 1)

        @block.gpsimd
        def _(pool):
            step = Steps(pool, pool_step)
            ta = rope_tmp[:, 0:SLAB].rearrange("p (c f) -> p c f", f=DK // 2)
            tb = rope_tmp[:, SLAB:2 * SLAB].rearrange("p (h c f) -> p h c f", c=2, f=DK // 2)
            pool.wait_ge(const_landed, CONSTS)
            for n in range(2):
                pool.wait_ge(bank_free, 4 * (n + 1) + 4)
                for t in range(NB):
                    x = rows[:, t, n * Q_DIM:(n + 1) * Q_DIM]
                    xc = x.rearrange("p (c f) -> p c f", f=DK // 2)
                    xh = x.rearrange("p (h c f) -> p h c f", c=2, f=DK // 2)
                    th = rope_tmp[:, 0:SLAB].rearrange("p (h c f) -> p h c f", c=2, f=DK // 2)
                    full, part = [P, 2 * HEADS, DK // 2], [P, HEADS, DK // 2]
                    cos, sin = rope[:, t, 0, :].unsqueeze(1), rope[:, t, 1, :].unsqueeze(1)
                    pool.tensor_tensor(ta, xc, cos.to_broadcast(full), ALU.mult)
                    pool.tensor_tensor(tb[:, :, 0, :], xh[:, :, 1, :], sin.to_broadcast(part), ALU.mult)
                    step(pool.tensor_tensor(tb[:, :, 1, :], xh[:, :, 0, :], sin.to_broadcast(part), ALU.mult))
                    pool.tensor_tensor(xh[:, :, 0, :], th[:, :, 0, :], tb[:, :, 0, :], ALU.subtract)
                    step(pool.tensor_tensor(xh[:, :, 1, :], th[:, :, 1, :], tb[:, :, 1, :], ALU.add))
                    pool.sem_inc(rope_done, 1)
            pool.wait_ge(silu_done, NB)
            for t in range(NB):
                pool.wait_ge(y_normed, t + 1)
                pool.tensor_tensor(rows[:, t, G0:G0 + V_DIM], rows[:, t, G0:G0 + V_DIM], rows[:, t, V0:V0 + V_DIM], ALU.mult)\
                    .then_inc(ret_ready, 1)
            for f in range(8):
                j, t, h = f // 4, (f // 2) % 2, f % 2
                col = j * SLAB + h * HALF
                pool.wait_ge(bank_free, 4 * (S_POOL + 1) + f + 1)
                pool.tensor_tensor(rows[:, t, col:col + HALF], rows[:, t, col:col + HALF], rows[:, t, D + col:D + col + HALF],
                                   ALU.add).then_inc(mixed_ready, 1)

            def take_idx(u, idx, slot, free, ring):
                pool.wait_ge(free, u * TOPK + ring)
                step_at(u, pool.tensor_copy(idx[:, slot, :], expert[:, bass.ds(u, 1), :].rearrange("p u k -> p (u k)")))

            def gather(table, ring, landed, free, idx, u, slot, k):
                r = k % ring.shape[1]
                pool.wait_ge(free, u * TOPK + (AHEAD + k + 1))
                pool.sem_inc(pool_passed, 1)
                pool.indirect_dma_start(
                    out=ring[:, r, :], out_offset=None, in_=table,
                    in_offset=bass.IndirectOffsetOnAxis(ap=idx[:, slot, k:k + 1], axis=0),
                ).then_inc(landed[r], 16)

            base = [step.n]

            def step_at(u, ins):
                ins.then_inc(pool_step, 1)
                pool.wait_ge(pool_step, u + (base[0] + 1))
                pool.sem_inc(pool_passed, 1)

            def gathers_u(u, slot, first_block_tokens):
                take_idx(u, idx_u, slot, u_free, U_RING)
                for k in range(TOPK):
                    gather(a["peer_u"], u_ring, u_landed, u_free, idx_u, u, slot, k)
                    if first_block_tokens is not None and k >= U_RING and k % 3 == 1:
                        i, n0 = first_block_tokens, (k - U_RING) // 3 * 4
                        if n0 == 0:
                            pool.wait_ge(picks_ready, 1)
                            step2(i, pool.tensor_copy(pick_now[:, :, :], pick[:, :, bass.ds(i * TOPK, TOPK)]))
                        for n in range(n0, n0 + 4):
                            pool.wait_ge(onehot_free, i * TOPK + n + 1)
                            pool.sem_inc(pool_passed, 1)
                            pool.tensor_scalar(onehot[:, n % PICK_RING, 0, :], iota[:, :], pick_now[:, 0, n:n + 1], None,
                                               ALU.is_equal)
                            pool.tensor_scalar(onehot[:, n % PICK_RING, 1, :], iota[:, :], pick_now[:, 1, n:n + 1],
                                               pick_now[:, 2, n:n + 1], ALU.is_equal, ALU.mult).then_inc(onehot_ready, 1)

            def step2(i, ins):
                ins.then_inc(pick_copied, 1)
                pool.wait_ge(pick_copied, i + 1)
                pool.sem_inc(pool_passed, 1)

            def units_u(u0, n, found, tokens=False):
                pool.wait_ge(topk_done, found)
                with pool.Fori(u0 // 2, (u0 + n) // 2) as i:
                    for m in range(2):
                        gathers_u(2 * i + m, m, 2 * i + (m - PEER_HEADS) if tokens else None)

            found_after = lambda j, b, h: j * 2 * HEADS_PER_SLAB + b * HEADS_PER_SLAB + h
            units_u(0, 2, found_after(0, 0, 2))
            units_u(2, 2, found_after(0, 0, 4))
            units_u(4, 4, found_after(1, 0, 4))
            units_u(8, 8, found_after(1, 1, 4), True)

            base[0] += UNITS
            upper = a["peer_v"].rearrange("e (s c) -> (e s) c", s=2)
            pool.wait_ge(rows_ready, 2 * NB)
            with pool.Fori(0, UNITS // 2) as i:
                for m in range(2):
                    u = 2 * i + m
                    take_idx(u, idx_v, m, v_free, V_RING)
                    pool.tensor_scalar(idx_v[:, m, :], idx_v[:, m, :], 2.0, 1.0, ALU.mult, ALU.add).then_inc(idx_doubled, 1)
                    pool.wait_ge(idx_doubled, u + 1)
                    for k in range(TOPK):
                        gather(upper, v_ring, v_landed, v_free, idx_v, u, m, k)


def kernel(x, norm1_w, w_in, w_ret_o, w_pool_lin, pool_scale, w_pool_o, w_out, norm2_w, peer_w_q,
           peer_sub_keys, peer_u, peer_v, final_norm_w):
    import concourse.bacc as bacc
    from concourse.bass_utils import run_bass_kernel_spmd

    host = {
        "x": x[0], "norm1_w": norm1_w[0], "w_in": w_in[0], "w_ret_o": w_ret_o[0], "w_pool_lin": w_pool_lin[0],
        "pool_scale": np.asarray(pool_scale)[0].reshape(POOL_KC, P).T,
        "w_pool_o": w_pool_o[0], "w_out": w_out[0], "norm2_w": norm2_w[0], "peer_w_q": peer_w_q[0],
        "peer_sub_keys": np.asarray(peer_sub_keys)[0].transpose(2, 0, 1).reshape(P, 2 * NKEYS),
        "peer_u": peer_u[0], "peer_v": peer_v[0], "final_norm_w": final_norm_w,
    }
    host.update(constants())
    nc = bacc.Bacc("TRN2", target_bir_lowering=False, num_devices=1)
    arrays, aps = {}, {}
    for name, value in host.items():
        value = np.ascontiguousarray(value)
        arrays[f"in_{name}"] = value
        aps[name] = nc.dram_tensor(f"in_{name}", value.shape, mybir.dt.from_np(value.dtype), kind="ExternalInput").ap()
    out = nc.dram_tensor("out_dram", (SEQ, D), F32, kind="ExternalOutput").ap()
    build(nc, aps, out)
    r = run_bass_kernel_spmd(nc, [arrays], core_ids=[0])
    return r.results[0]["out_dram"].reshape(1, SEQ, D)
```

```python
from contextlib import ExitStack

import numpy as np

import concourse.bass as bass
from concourse import mybir

F32 = mybir.dt.float32
F32R = mybir.dt.float32r
BF16 = mybir.dt.bfloat16
U32 = mybir.dt.uint32
ALU = mybir.AluOpType
ACT = mybir.ActivationFunctionType
AX_X = mybir.AxisListType.X

P = 128
D = 2048
SEQ = 256
NB = SEQ // P
KC = D // P
HEADS, DK, DV = 8, 128, 256
Q_DIM, V_DIM = HEADS * DK, HEADS * DV
POOL_WINDOWS = (2, 4, 8, 16)
POOL_GROUPS, POOL_DIM = len(POOL_WINDOWS), 1024
POOL_GDIM = POOL_DIM // POOL_GROUPS
POOL_KC = POOL_DIM // P
PEER_HEADS, NKEYS, TOPK = 8, 128, 16
EPS = 1e-6
ROPE_BASE = 10000.0
NEG = -3.0e38

SLAB = 1024
HALF = 512
BANKS = NB * (SLAB // HALF)

Q0, K0, V0 = 0, Q_DIM, 2 * Q_DIM
G0 = V0 + V_DIM
P0 = G0 + V_DIM
GATE0 = P0 + POOL_DIM
MIX_COLS = GATE0
MIX_SLABS = MIX_COLS // SLAB
GATE_SLABS = 2 * D // SLAB
D_SLABS = D // SLAB
S_MIX = 0
S_GATE = S_MIX + MIX_SLABS
S_RET = S_GATE + GATE_SLABS
S_POOL = S_RET + D_SLABS
S_OUT = S_POOL + D_SLABS
S_Q = S_OUT + D_SLABS
S_END = S_Q + D_SLABS


def groups_at(i):
    n = i - (PICK_UNITS * TOPK - PICK_DOTS)
    return range(max(n, 0) * GROUPS // PICK_DOTS, max(n + 1, 0) * GROUPS // PICK_DOTS)


def first_tile(slab):
    short = min(max(slab - S_POOL, 0), D_SLABS)
    return slab * KC - short * (KC - POOL_KC)


W_RING = 4
EARLY = 4
LEAD = W_RING - 1
G_RING = 4
T_RING = 8
T_LAST = T_RING // 2
E_RING = 4
UNITS = NB * PEER_HEADS
HEADS_PER_SLAB = SLAB // (2 * NKEYS)
HALF_D = D // 2
LOW_KC = HALF_D // P
GROUP = 4
GROUPS = SEQ // GROUP
PICK_UNITS = 4
PICK_DOTS = 44
POOL_TOKENS = 1
GATHERS_AHEAD = 1
SPREAD_UNITS = GROUPS // TOPK
SCORE_KEYS = UNITS * 2 * NKEYS // SEQ
ROOM_KEYS = NKEYS - SCORE_KEYS - NB * SLAB // SEQ - T_LAST * HALF // SEQ


def constants():
    half = DK // 2
    inv_freq = (ROPE_BASE ** (-np.arange(half, dtype=np.float32) / half)).astype(np.float32)
    ang = np.arange(SEQ, dtype=np.float32)[:, None] * inv_freq[None, :]
    rope = np.stack([np.cos(ang), np.sin(ang)], 1).astype(np.float32)
    log_g = np.log(1.0 - 2.0 ** (-5.0 - np.arange(HEADS, dtype=np.float64)))
    diff = np.arange(SEQ)[None, :] - np.arange(P)[:, None]
    decay = np.where(diff[:, None] >= 0, np.exp(log_g[None, :, None] * np.maximum(diff, 0)[:, None]), 0.0)
    decay = decay * DK ** -0.5
    mask = decay.astype(np.float32)
    band = np.zeros((NB, P, POOL_GROUPS, SEQ), np.float32)
    for g, w in enumerate(POOL_WINDOWS):
        for t in range(SEQ):
            lo = max(0, t - w + 1)
            for s in range(lo, t + 1):
                band[s // P, s % P, g, t] = 1.0 / (t + 1 - lo) - (1.0 if s == t else 0.0)
    band = np.ascontiguousarray(band.transpose(1, 2, 0, 3))
    return {
        "rope": rope,
        "mask": mask.reshape(P, -1),
        "band": band.reshape(P, -1),
        "ident": np.eye(P, dtype=np.float32),
        "iota": np.tile(np.arange(NKEYS, dtype=np.float32), (P, 1)),
    }


def build(nc, a, out):
    with ExitStack() as ctx:
        def sb(name, shape, dt=F32):
            return ctx.enter_context(nc.sbuf_tensor(name, shape, dt))

        def sem(name):
            return ctx.enter_context(nc.semaphore(name))

        x_sb = sb("x_sb", [P, NB, D])
        rope_gate = sb("rope_gate", [P, 256])
        ident = sb("ident_sb", [P, P])
        iota = sb("iota_sb", [P, NKEYS])
        zeros = sb("zeros", [P, P])
        pscale = sb("pscale_sb", [P, POOL_KC])
        final_w = sb("final_w", [P, D])
        keys_hi = sb("keys_hi", [P, 2, NKEYS], F32R)
        keys_lo = sb("keys_lo", [P, 2, NKEYS], F32R)
        qk_tmp = sb("qk_tmp", [P, 1024])
        probs_picks = sb("probs_picks", [P, 1024])
        stat = sb("stat", [P, 2 * HEADS, 6])
        mean_var = sb("mean_var", [P, 2 * HEADS, 2])
        norm_a = sb("norm_a", [P, 2 * HEADS])
        norm_b = sb("norm_b", [P, 2 * HEADS])
        norm_c = sb("norm_c", [P, 2 * HEADS])
        row_scale = sb("row_scale", [P, 3, NB])
        top_val = sb("top_val", [P, 2, TOPK])
        top_idx = sb("top_idx", [P, 2, TOPK], U32)
        best = sb("best", [P, TOPK])
        best_pos = sb("best_pos", [P, TOPK], U32)
        pos_ab = sb("pos_ab", [P, 2, TOPK], U32)
        expert_ab = sb("expert_ab", [P, 2, TOPK])
        expert = sb("expert", [P, UNITS, TOPK], U32)
        ident_bf = sb("ident_bf", [P, P], BF16)
        weight = sb("weight", [P, UNITS, TOPK])
        idx = sb("idx", [P, 2, TOPK], U32)
        dots = sb("dots", [P, UNITS, TOPK])
        dots_now = sb("dots_now", [P, 2, TOPK])
        gate_sum = sb("gate_sum", [P, 2, UNITS])
        pick = sb("pick", [P, 3, SEQ])
        second_bf = sb("second_bf", [P, 2, GROUP * P], BF16)

        rope = rope_gate[:, :].rearrange("p (t c f) -> p t c f", t=NB, c=2)
        gate = rope_gate[:, :].rearrange("p (u k) -> p u k", u=UNITS)
        keys_raw = expert[:, :, :].bitcast(F32).rearrange("p u k -> p (u k)").rearrange("p (h k) -> p h k", h=2)
        qk_t = qk_tmp[:, :].rearrange("p (r n t) -> p r n t", r=2, n=4)
        tmp_a, tmp_b = qk_tmp[:, 0:512], qk_tmp[:, 512:768]
        staged = qk_tmp[:, :].rearrange("p (r t) -> p r t", r=E_RING)
        keys_t = qk_tmp[:, :].rearrange("p (m t) -> p m t", m=2)
        probs = probs_picks[:, 0:768].rearrange("p (r t) -> p r t", r=2)
        first_hot = probs_picks[:, :].rearrange("p (m n k) -> p m n k", m=2, n=GROUP)
        second_hot = qk_tmp[:, :].rearrange("p (m t) -> p m t", m=2)
        pick_int = probs_picks[:, 0:3 * SEQ].bitcast(U32).rearrange("p (n t) -> p n t", n=3)
        expert_f = probs_picks[:, 3 * SEQ:4 * SEQ]
        low_dots = probs_picks[:, 2 * SEQ:3 * SEQ]
        h2_t = final_w[:, :].rearrange("p (k t) -> p k t", k=LOW_KC)

        with ExitStack() as lay:
            def first(name, shape, dt=F32):
                return lay.enter_context(nc.sbuf_tensor(name, shape, dt))

            act_hi = first("act_hi", [P, KC, SEQ], F32R)
            act_lo = first("act_lo", [P, KC, SEQ], F32R)
            pact_hi = first("pact_hi", [P, POOL_KC, SEQ], F32R)
            pact_lo = first("pact_lo", [P, POOL_KC, SEQ], F32R)
            w_hi = first("w_hi", [P, W_RING, SLAB], F32R)
            w_lo = first("w_lo", [P, W_RING, SLAB], F32R)
            w_raw = first("w_raw", [P, W_RING, SLAB])
            rows = first("rows", [P, NB, MIX_COLS])
            w_lin = first("w_lin", [P, POOL_GROUPS, 2, POOL_GDIM])
        with ExitStack() as lay:
            lay.enter_context(nc.sbuf_tensor("under_tables", [P, 2 * KC * SEQ], F32))
            mask = lay.enter_context(nc.sbuf_tensor("mask_sb", [P, HEADS, SEQ], F32))
            band = lay.enter_context(nc.sbuf_tensor("band_sb", [P, POOL_GROUPS, NB, SEQ], F32))
        with ExitStack() as lay:
            lay.enter_context(nc.sbuf_tensor("under_t_extra", [P, ROOM_KEYS * SEQ], F32))
            t_extra = lay.enter_context(nc.sbuf_tensor("t_extra", [P, T_RING - T_LAST, HALF], F32))
            q_rows = lay.enter_context(nc.sbuf_tensor("q_rows", [P, NB, SLAB], F32))
            scores = lay.enter_context(nc.sbuf_tensor("scores", [P, D_SLABS, NB, SLAB], F32))
        plane = sb("plane", [P, NKEYS, SEQ])
        h2 = sb("h2", [P, NB, D])
        v_room = sb("v_room", [P, G_RING, HALF_D])
        e_ring = h2[:, :, :].rearrange("p b (r c) -> p (b r) c", r=2)
        t_ring = [h2[:, r // 2, (r % 2) * HALF:(r % 2 + 1) * HALF] for r in range(T_LAST)]
        t_ring += [t_extra[:, r, :] for r in range(T_RING - T_LAST)]
        g_ring = v_room[:, :, :]
        h_rows = rows[:, :, 0:D]
        norm1 = rows[:, 0, D:2 * D]
        norm2 = v_room[:, 2:4, :].rearrange("p r c -> p (r c)")
        junk = v_room[:, 0:2, :].rearrange("p r c -> p (r c)")
        pooled = rows[:, 0, 0:2 * SLAB].rearrange("p (k t) -> p k t", k=POOL_KC)
        rope_tmp = rows[:, 0, G0:G0 + 2 * SLAB]

        bank = ctx.enter_context(nc.psum_tensor("bank", [P, BANKS, HALF], F32))
        misc = ctx.enter_context(nc.psum_tensor("misc", [P, 4, HALF], F32))

        x_landed = sem("x_landed")
        norm1_landed = sem("norm1_landed")
        const_landed = sem("const_landed")
        norm2_landed = sem("norm2_landed")
        final_landed = sem("final_landed")
        tile_landed = [sem(f"tile_landed{s}") for s in range(W_RING)]
        tile_hi = sem("tile_hi")
        tile_lo = sem("tile_lo")
        split_free = sem("split_free")
        bank_full = sem("bank_full")
        bank_free = sem("bank_free")
        squares_done = sem("squares_done")
        norm_step = sem("norm_step")
        root_done = sem("root_done")
        scale_ready = sem("scale_ready")
        rows_ready = sem("rows_ready")
        turned = sem("turned")
        turned_hi = sem("turned_hi")
        turned_lo = sem("turned_lo")
        rope_done = sem("rope_done")
        qk_turned = sem("qk_turned")
        qk_copied = sem("qk_copied")
        scores_full = sem("scores_full")
        probs_ready = sem("probs_ready")
        y_full = sem("y_full")
        y_copied = sem("y_copied")
        pooled_full = sem("pooled_full")
        pooled_copied = sem("pooled_copied")
        lin_full = sem("lin_full")
        lin_hi = sem("lin_hi")
        lin_lo = sem("lin_lo")
        silu_done = sem("silu_done")
        y_normed = sem("y_normed")
        ret_ready = sem("ret_ready")
        mixed_ready = sem("mixed_ready")
        resid_ready = sem("resid_ready")
        keys_hi_done = sem("keys_hi_done")
        keys_split = sem("keys_split")
        q_turned = sem("q_turned")
        q_hi = sem("q_hi")
        q_lo = sem("q_lo")
        key_scores = sem("key_scores")
        topk_done = sem("topk_done")
        scores_copied = sem("scores_copied")
        exp_done = sem("exp_done")
        g_landed = [sem(f"g_landed{s}") for s in range(G_RING)]
        t_landed = [sem(f"t_landed{s}") for s in range(T_RING)]
        e_landed = [sem(f"e_landed{s}") for s in range(E_RING)]
        g_free = sem("g_free")
        t_free = sem("t_free")
        low_full = sem("low_full")
        low_copied = sem("low_copied")
        e_free = sem("e_free")
        ident_ready = sem("ident_ready")
        experts_flat = sem("experts_flat")
        experts_turned = sem("experts_turned")
        picks_ready = sem("picks_ready")
        second_ready = sem("second_ready")
        pool_ready = sem("pool_ready")
        first_ready = sem("first_ready")
        hot_free = sem("hot_free")
        keys_copied = sem("keys_copied")
        picked_full = sem("picked_full")
        picked_read = sem("picked_read")
        low_summed = sem("low_summed")
        dots_turned = sem("dots_turned")
        dots_whole = sem("dots_whole")
        gelu_done = sem("gelu_done")
        weighted = sem("weighted")
        weights_turned = sem("weights_turned")
        weights_ready = sem("weights_ready")
        spread_copied = sem("spread_copied")
        staged_ready = sem("staged_ready")
        y_peer_full = sem("y_peer_full")
        zeros_ready = sem("zeros_ready")
        dve_step = sem("dve_step")
        act_step = sem("act_step")
        pool_step = sem("pool_step")
        final_weighted = sem("final_weighted")
        final_ready = [sem(f"final_ready{b}") for b in range(NB)]
        idx_copied = sem("idx_copied")
        pool_passed = sem("pool_passed")
        stored = sem("stored")

        AHEAD = TOPK

        const_loads = [
            (keys_raw, a["peer_sub_keys"].rearrange("d (p k) -> d p k", p=2)),
            (rope, a["rope"].rearrange("(t p) c f -> p t c f", p=P)),
            (iota[:, :], a["iota"]),
            (pscale[:, :], a["pool_scale"]),
            (mask[:, :, :], a["mask"].rearrange("p (h t) -> p h t", h=HEADS)),
            (band[:, :, :, :], a["band"].rearrange("p (g s t) -> p g s t", g=POOL_GROUPS, s=NB)),
            (w_lin[:, :, :, :], a["w_pool_lin"].rearrange("g (c p) d -> p g c d", p=P)),
        ]
        CONSTS = 16 * len(const_loads)

        class Steps:

            def __init__(self, eng, semaphore):
                self.eng, self.sem, self.n = eng, semaphore, 0

            def __call__(self, ins):
                self.n += 1
                ins.then_inc(self.sem, 1)
                self.eng.wait_ge(self.sem, self.n)

        block = ctx.enter_context(nc.Block())

        @block.sync
        def _(sp):
            sp.dma_start(x_sb[:, :, :], a["x"].rearrange("(t p) d -> p t d", p=P)).then_inc(x_landed, 16)
            sp.dma_start(norm1, a["norm1_w"].rearrange("(o d) -> o d", o=1).to_broadcast([P, D])).then_inc(norm1_landed, 16)

            def slab_tiles(w, col, t0, kc):
                for k in range(kc):
                    if not (isinstance(t0, int) and t0 + k < W_RING):
                        sp.wait_ge(tile_lo, t0 + (k + 1 - W_RING))
                    sp.dma_start(w_raw[:, k % W_RING, :], w[k * P:(k + 1) * P, bass.ds(col, SLAB)])\
                        .then_inc(tile_landed[k % W_RING], 16)

            sp.dma_start(ident[:, :], a["ident"]).then_inc(x_landed, 16)
            slab_tiles(a["w_in"], 0, 0, KC)
            for dst, src in const_loads:
                sp.dma_start(dst, src).then_inc(const_landed, 16)
            with sp.Fori(1, MIX_SLABS + GATE_SLABS) as j:
                slab_tiles(a["w_in"], j * SLAB, j * KC, KC)
            with sp.Fori(0, D_SLABS) as j:
                slab_tiles(a["w_ret_o"], j * SLAB, first_tile(S_RET) + j * KC, KC)
            sp.wait_ge(lin_full, POOL_GROUPS)
            sp.dma_start(norm2, a["norm2_w"].rearrange("(o d) -> o d", o=1).to_broadcast([P, D])).then_inc(norm2_landed, 16)
            with sp.Fori(0, D_SLABS) as j:
                slab_tiles(a["w_pool_o"], j * SLAB, first_tile(S_POOL) + j * POOL_KC, POOL_KC)
            with sp.Fori(0, D_SLABS) as j:
                slab_tiles(a["w_out"], j * SLAB, first_tile(S_OUT) + j * KC, KC)
            with sp.Fori(0, D_SLABS) as j:
                slab_tiles(a["peer_w_q"], j * SLAB, first_tile(S_Q) + j * KC, KC)
            sp.wait_ge(turned, 32)
            for first, last, ring in ((0, ROOM_KEYS, T_RING), (ROOM_KEYS, NKEYS, T_LAST)):
                with sp.Fori(first // BANKS, last // BANKS) as i:
                    for n in range(BANKS):
                        for s in range(2):
                            sp.wait_ge((t_free, low_full)[s], BANKS * i + (n + 1 + (T_RING - ring) // 2))
                            r = (2 * n + s) % ring
                            sp.dma_start(t_ring[r], a["peer_u_low"][:, bass.ds((BANKS * i + n) * SLAB + s * HALF, HALF)])\
                                .then_inc(t_landed[r], 16)
            sp.wait_ge(low_full, BANKS + NKEYS)
            sp.dma_start(final_w[:, :], a["final_norm_w"].rearrange("(o d) -> o d", o=1).to_broadcast([P, D])).then_inc(final_landed, 16)
            sp.wait_ge(g_free, AHEAD + G_RING + UNITS * TOPK)
            with sp.Fori(0, NKEYS // E_RING) as i:
                for r in range(E_RING):
                    sp.wait_ge(e_free, i * E_RING + r + 1)
                    sp.dma_start(e_ring[:, r, :], a["peer_v"][bass.ds((i * E_RING + r) * P, P), 0:HALF_D])\
                        .then_inc(e_landed[r], 16)
            for b in range(NB):
                sp.wait_ge(final_ready[b], 1)
                sp.dma_start(out[b * P:(b + 1) * P, :], h2[:, b, :]).then_inc(stored, 16)
            sp.wait_ge(stored, 16 * NB)

        @block.tensor
        def _(pe):
            pe.sem_inc(split_free, W_RING)
            pe.sem_inc(e_free, E_RING)
            pe.sem_inc(hot_free, 2)
            pe.sem_inc(t_free, BANKS)
            pe.sem_inc(low_full, BANKS)
            pe.sem_inc(picked_full, 2)

            def slab(s, t0, kc, hi, lo):
                for k in range(kc):
                    r = k % W_RING
                    pe.wait_ge(tile_lo, t0 + k + 1)
                    for t in range(NB):
                        for h in range(2):
                            b = 2 * t + h
                            if k == 0:
                                pe.wait_ge(bank_free, 4 * s + b + 1)
                            o = bank[:, b, :]
                            rh, rl = w_hi[:, r, h * HALF:(h + 1) * HALF], w_lo[:, r, h * HALF:(h + 1) * HALF]
                            lh, ll = hi[:, k, t * P:(t + 1) * P], lo[:, k, t * P:(t + 1) * P]
                            pe.matmul(o, lh, rh, start=(k == 0), stop=False)
                            pe.matmul(o, lh, rl, start=False, stop=False)
                            m = pe.matmul(o, ll, rh, start=False, stop=(k == kc - 1))
                            if k == kc - 1:
                                m.then_inc(bank_full, 1)
                    (pe.drain() if k == kc - 1 else m).then_inc(split_free, 1)

            def turn(stage, src, ready):
                for f in range(8):
                    j, t, h = f // 4, (f // 2) % 2, f % 2
                    for s, n in ready(f):
                        pe.wait_ge(s, n)
                    if stage or f >= 4:
                        pe.wait_ge(turned_lo, 8 * stage + f - 3)
                    for c in range(4):
                        col = j * SLAB + h * HALF + c * P
                        m = pe.transpose(misc[:, f % 4, c * P:(c + 1) * P], src[:, t, col:col + P], ident[:, :])
                    m.then_inc(turned, 1)

            pe.wait_ge(x_landed, 32)
            turn(0, h_rows, lambda f: [(rows_ready, (f // 2) % 2 + 1)])
            pe.wait_ge(turned_lo, 8)
            with pe.Fori(0, MIX_SLABS) as j:
                slab(j, j * KC, KC, act_hi, act_lo)

            pe.wait_ge(rope_done, 2 * NB)
            for i in range(HEADS + 2):
                if i < HEADS:
                    h = i
                    if h >= 2:
                        pe.wait_ge(qk_copied, h - 1)
                    for n in range(4):
                        col = (Q0 if n < 2 else K0) + h * DK
                        m = pe.transpose(misc[:, h % 2, n * P:(n + 1) * P], rows[:, n % 2, col:col + DK], ident[:, :])
                    m.then_inc(qk_turned, 1)
                if 1 <= i <= HEADS:
                    h = i - 1
                    pe.wait_ge(qk_copied, h + 1)
                    if h >= 1:
                        pe.wait_ge(probs_ready, h)
                    q = qk_t[:, h % 2, 0:2, :].rearrange("p n t -> p (n t)")
                    pe.matmul(misc[:, 2, 0:2 * P], qk_t[:, h % 2, 2, :], q, start=True, stop=True)
                    pe.matmul(misc[:, 2, 2 * P:3 * P], qk_t[:, h % 2, 3, :], qk_t[:, h % 2, 1, :],
                              start=True, stop=True).then_inc(scores_full, 1)
                if i >= 2:
                    h = i - 2
                    pe.wait_ge(probs_ready, h + 1)
                    if h == 0:
                        pe.wait_ge(bank_free, 4 * MIX_SLABS)
                    else:
                        pe.wait_ge(y_copied, h)
                    v = [rows[:, t, V0 + h * DV:V0 + (h + 1) * DV] for t in range(NB)]
                    pr = probs[:, h % 2, :]
                    pe.matmul(misc[:, 3, 0:DV], pr[:, 0:P], v[0], start=True, stop=True)
                    pe.matmul(misc[:, 3, DV:2 * DV], pr[:, P:2 * P], v[0], start=True, stop=False)
                    pe.matmul(misc[:, 3, DV:2 * DV], pr[:, 2 * P:3 * P], v[1], start=False, stop=True)\
                        .then_inc(y_full, 1)

            pe.wait_ge(const_landed, CONSTS)
            pe.wait_ge(bank_free, 4 * MIX_SLABS + 4)
            pe.wait_ge(y_copied, HEADS)
            for f in range(POOL_GROUPS):
                for c in range(2):
                    col = P0 + (2 * f + c) * P
                    o = misc[:, f, c * SEQ:(c + 1) * SEQ]
                    pe.matmul(o, rows[:, 0, col:col + P], band[:, f, 0, :], start=True, stop=False)
                    m = pe.matmul(o, rows[:, 1, col:col + P], band[:, f, 1, :], start=False, stop=True)
                m.then_inc(pooled_full, 1)
            for f in range(POOL_GROUPS):
                pe.wait_ge(pooled_copied, f + 1)
                for d in range(2):
                    o = misc[:, f, d * SEQ:(d + 1) * SEQ]
                    for c in range(2):
                        m = pe.matmul(o, w_lin[:, f, c, d * P:(d + 1) * P], pooled[:, 2 * f + c, :],
                                      start=(c == 0), stop=(c == 1))
                m.then_inc(lin_full, 1)

            with pe.Fori(S_GATE, S_RET) as j:
                slab(j, j * KC, KC, act_hi, act_lo)

            pe.wait_ge(lin_lo, POOL_GROUPS)
            turn(1, rows[:, :, G0:G0 + D], lambda f: [(ret_ready, (f // 2) % 2 + 1)])
            pe.wait_ge(turned_lo, 16)
            with pe.Fori(0, D_SLABS) as j:
                slab(S_RET + j, first_tile(S_RET) + j * KC, KC, act_hi, act_lo)
            with pe.Fori(0, D_SLABS) as j:
                slab(S_POOL + j, first_tile(S_POOL) + j * POOL_KC, POOL_KC, pact_hi, pact_lo)

            turn(2, rows[:, :, 0:D], lambda f: [(mixed_ready, f + 1)])
            pe.wait_ge(turned_lo, 24)
            with pe.Fori(0, D_SLABS) as j:
                slab(S_OUT + j, first_tile(S_OUT) + j * KC, KC, act_hi, act_lo)

            turn(3, h2, lambda f: [(rows_ready, 2 + (f // 2) % 2 + 1)])
            pe.wait_ge(turned_lo, 32)
            pe.wait_ge(keys_split, 1)
            for j in range(D_SLABS):
                slab(S_Q + j, first_tile(S_Q + j), KC, act_hi, act_lo)
                if j:
                    pe.wait_ge(scores_copied, NB * j)
                for f in range(4):
                    t, g = f // 2, f % 2
                    pe.wait_ge(bank_free, 4 * (S_Q + j) + BANKS + f + 1)
                    for c in range(4):
                        m = pe.transpose(misc[:, f, c * P:(c + 1) * P],
                                         q_rows[:, t, (4 * g + c) * P:(4 * g + c + 1) * P], ident[:, :])
                    m.then_inc(q_turned, 1)
                pe.wait_ge(q_lo, 4 * (j + 1))
                for t in range(NB):
                    for c in range(8):
                        o = misc[:, 2 * t + c // 4, (c % 4) * P:(c % 4 + 1) * P]
                        lh, ll = pact_hi[:, c, t * P:(t + 1) * P], pact_lo[:, c, t * P:(t + 1) * P]
                        rh, rl = keys_hi[:, c % 2, :], keys_lo[:, c % 2, :]
                        pe.matmul(o, lh, rh, start=True, stop=False)
                        pe.matmul(o, lh, rl, start=False, stop=False)
                        m = pe.matmul(o, ll, rh, start=False, stop=True)
                    m.then_inc(key_scores, 1)

            pe.wait_ge(bank_free, 4 * S_END + BANKS)
            for first, last, ring in ((0, ROOM_KEYS, T_RING), (ROOM_KEYS, NKEYS, T_LAST)):
                with pe.Fori(first // BANKS, last // BANKS) as i:
                    for n in range(BANKS):
                        pe.wait_ge(low_copied, i * BANKS + n + 1)
                        for s in range(2):
                            r = (2 * n + s) % ring
                            per_round = 2 * BANKS // ring
                            before = first // BANKS * (1 - per_round)
                            pe.wait_ge(t_landed[r], (i * per_round + (before + (2 * n + s) // ring + 1)) * 16)
                            for k in range(LOW_KC // 2):
                                m = pe.matmul(bank[:, n, 0:SEQ], t_ring[r][:, k * P:(k + 1) * P], h2_t[:, s * LOW_KC // 2 + k, :],
                                              start=(s == 0 and k == 0), stop=(s == 1 and k == LOW_KC // 2 - 1))
                            m.then_inc((t_free, low_full)[s], 1)
            pe.wait_ge(experts_flat, 1)
            pe.wait_ge(low_copied, BANKS + NKEYS)
            for b in range(NB):
                m = pe.transpose(bank[:, 0, b * P:(b + 1) * P], expert_f[:, b * P:(b + 1) * P], ident[:, :])
            m.then_inc(experts_turned, 1)

            def turn_keys(g, m):
                pe.wait_ge(keys_copied, g + 1)
                pe.wait_ge(second_ready, g + 1)
                pe.wait_ge(pool_ready, g + 1)
                for n in range(GROUP):
                    i = pe.matmul(misc[:, m, n * P:(n + 1) * P], second_bf[:, m, n * P:(n + 1) * P], ident_bf[:, :],
                                  start=True, stop=True)
                i.then_inc(hot_free, 1)

            def pick_rows(g, m):
                pe.wait_ge(keys_copied, g + 3)
                pe.wait_ge(picked_read, g + 1)
                for n in range(GROUP):
                    i = pe.matmul(misc[:, 2 + m, n * P:(n + 1) * P], keys_t[:, m, n * P:(n + 1) * P],
                                  plane[:, :, bass.ds(g * GROUP + n, 1)].rearrange("p k o -> p (k o)"), start=True, stop=True)
                i.then_inc(picked_full, 1)

            pe.wait_ge(scores_copied, NB * D_SLABS)
            pe.wait_ge(ident_ready, 1)
            turn_keys(0, 0)
            with pe.Fori(0, GROUPS // 2 - 1) as i:
                for m in range(2):
                    turn_keys(2 * i + (m + 1), 1 - m)
                    pick_rows(2 * i + m, m)
            turn_keys(GROUPS - 1, 1)
            pick_rows(GROUPS - 2, 0)
            pick_rows(GROUPS - 1, 1)
            pe.wait_ge(low_summed, 1)
            for b in range(NB):
                m = pe.transpose(bank[:, 1, b * P:(b + 1) * P], low_dots[:, b * P:(b + 1) * P], ident[:, :])
            m.then_inc(dots_turned, 1)
            pe.wait_ge(weighted, 1)
            weight_flat = weight[:, :, :].rearrange("p u k -> p (u k)")
            for b in range(NB):
                m = pe.transpose(bank[:, 2, b * P:(b + 1) * P], weight_flat[:, b * P:(b + 1) * P], ident[:, :])
            m.then_inc(weights_turned, 1)

            with pe.Fori(0, GROUPS // 4) as i:
                for q in range(4):
                    pe.wait_ge(spread_copied, i * 4 + q + 1)
                    pe.wait_ge(second_ready, i * 4 + (GROUPS + q + 1))
                    pe.wait_ge(first_ready, i * 4 + q + 1)
                    for n in range(GROUP):
                        m = pe.matmul(misc[:, q, n * P:(n + 1) * P], second_hot[:, q % 2, n * P:(n + 1) * P],
                                      first_hot[:, q % 2, n, :], start=True, stop=True)
                    m.then_inc(hot_free, 1)

            pe.wait_ge(zeros_ready, 1)
            pe.wait_ge(weights_ready, 1)
            blank = zeros[:, :].unsqueeze(1).to_broadcast([P, HALF // P, P])
            for n in range(BANKS):
                pe.matmul(bank[:, n, :], zeros[:, :], blank, start=True, stop=False, skip_group_check=True)
            with pe.Fori(0, NKEYS // E_RING) as i:
                for r in range(E_RING):
                    pe.wait_ge(staged_ready, i * E_RING + r + 1)
                    pe.wait_ge(e_landed[r], i * 16 + 16)
                    for b in range(NB):
                        for h in range(2):
                            m = pe.matmul(bank[:, 2 * b + h, :], staged[:, r, b * P:(b + 1) * P], e_ring[:, r, h * HALF:(h + 1) * HALF],
                                          start=False, stop=False, skip_group_check=True)
                    m.then_inc(e_free, 1)
            for n in range(BANKS):
                m = pe.matmul(bank[:, n, :], zeros[:, :], blank, start=False, stop=True, skip_group_check=True)
            m.then_inc(y_peer_full, 1)

        @block.scalar
        def _(act):
            act.sem_inc(bank_free, BANKS)
            act.sem_inc(spread_copied, 4)
            act.sem_inc(low_copied, BANKS)
            act.sem_inc(keys_copied, 2)
            step = Steps(act, act_step)

            def tiles(t0, k0, n):
                for k in range(k0, k0 + n):
                    r = k % W_RING
                    act.wait_ge(split_free, t0 + k + 1)
                    act.wait_ge(tile_landed[r], landed(t0, k))
                    act.activation(w_hi[:, r, :], w_raw[:, r, :], ACT.Copy).then_inc(tile_hi, 1)

            def landed(t0, k):
                return t0 * (16 // W_RING) + 16 * (k // W_RING + 1)

            def turned_high(stage):
                for f in range(8):
                    n = 8 * stage + f + 1
                    j, t, h = f // 4, (f // 2) % 2, f % 2
                    c = (j * SLAB + h * HALF) // P
                    act.wait_ge(turned, n)
                    if stage == 3 and j == 0:
                        act.activation(h2_t[:, c:c + 4, t * P:(t + 1) * P],
                                       misc[:, f % 4, :].rearrange("p (c t) -> p c t", c=4), ACT.Copy)
                    act.activation(act_hi[:, c:c + 4, t * P:(t + 1) * P],
                                   misc[:, f % 4, :].rearrange("p (c t) -> p c t", c=4), ACT.Copy).then_inc(turned_hi, 1)

            def squares():
                for t in range(NB):
                    step(act.activation(junk, x_sb[:, t, :], ACT.Square, accum_out=norm_a[:, t:t + 1]))
                act.sem_inc(squares_done, 1)

            def root(n0):
                act.wait_ge(norm_step, n0)
                act.activation(norm_c[:, 0:NB], norm_b[:, 0:NB], ACT.Sqrt).then_inc(root_done, 1)

            act.wait_ge(x_landed, 32)
            squares()
            root(1)
            act.activation(ident_bf[:, :], ident[:, :], ACT.Copy).then_inc(ident_ready, 1)
            tiles(0, 0, LEAD)
            turned_high(0)
            act.wait_ge(scale_ready, 1)
            for first, last in ((0, G0 // SLAB), (G0 // SLAB, MIX_SLABS)):
                if first:
                    act.wait_ge(rope_done, 2 * NB)
                with act.Fori(first, last) as j:
                    tiles(j * KC, LEAD, KC)
                    for b in range(BANKS):
                        act.wait_ge(bank_full, 4 * j + b + 1)
                        act.activation(rows[:, b // 2, bass.ds(j * SLAB + (b % 2) * HALF, HALF)], bank[:, b, :], ACT.Copy,
                                       scale=row_scale[:, 0, b // 2:b // 2 + 1]).then_inc(bank_free, 1)
            for i in range(HEADS + 2):
                if i < HEADS:
                    act.wait_ge(qk_turned, i + 1)
                    if i >= 2:
                        act.wait_ge(scores_full, i - 1)
                    act.activation(qk_t[:, i % 2, :, :].rearrange("p n t -> p (n t)"), misc[:, i % 2, :], ACT.Copy)\
                        .then_inc(qk_copied, 1)
                if i >= 2:
                    h = i - 2
                    act.wait_ge(y_full, h + 1)
                    act.activation(rows[:, :, V0 + h * DV:V0 + (h + 1) * DV],
                                   misc[:, 3, :].rearrange("p (t c) -> p t c", t=NB), ACT.Copy).then_inc(y_copied, 1)
            for f in range(POOL_GROUPS):
                act.wait_ge(pooled_full, f + 1)
                act.activation(pooled[:, 2 * f:2 * f + 2, :].rearrange("p k t -> p (k t)"), misc[:, f, :], ACT.Copy)\
                    .then_inc(pooled_copied, 1)
            for f in range(POOL_GROUPS):
                act.wait_ge(lin_full, f + 1)
                for d in range(2):
                    m = act.activation(pact_hi[:, 2 * f + d, :], misc[:, f, d * SEQ:(d + 1) * SEQ], ACT.Copy,
                                       scale=pscale[:, 2 * f + d:2 * f + d + 1])
                m.then_inc(lin_hi, 1)
            t_gate = first_tile(S_GATE)
            tiles(t_gate, LEAD, EARLY)
            for t in range(NB):
                act.activation(rows[:, t, G0:G0 + V_DIM], rows[:, t, G0:G0 + V_DIM], ACT.Silu).then_inc(silu_done, 1)
            tiles(t_gate, LEAD + EARLY, EARLY)
            act.wait_ge(norm_step, 2)
            act.activation(norm_c[:, :], norm_b[:, :], ACT.Sqrt).then_inc(root_done, 1)
            act.activation(keys_hi[:, :, :], keys_raw, ACT.Copy).then_inc(keys_hi_done, 1)
            tiles(t_gate, LEAD + 2 * EARLY, KC - 2 * EARLY)

            def gates(j):
                for b in range(BANKS):
                    act.wait_ge(bank_full, 4 * j + (4 * S_GATE + b + 1))
                    act.activation(rows[:, b // 2, bass.ds(j * SLAB + (b % 2) * HALF, HALF)], bank[:, b, :],
                                   ACT.Sigmoid, scale=row_scale[:, 0, b // 2:b // 2 + 1]).then_inc(bank_free, 1)

            gates(0)
            for first, last in ((1, V0 // SLAB), (V0 // SLAB, GATE_SLABS)):
                if first > 1:
                    act.wait_ge(ret_ready, NB)
                with act.Fori(first, last) as j:
                    tiles(j * KC + t_gate, LEAD, KC)
                    gates(j)
            turned_high(1)
            with act.Fori(0, D_SLABS) as j:
                tiles(j * KC + first_tile(S_RET), LEAD, KC)
            with act.Fori(0, D_SLABS) as j:
                tiles(j * POOL_KC + first_tile(S_POOL), LEAD, POOL_KC)
            turned_high(2)
            with act.Fori(0, D_SLABS) as j:
                tiles(j * KC + first_tile(S_OUT), LEAD, KC)
            act.wait_ge(bank_free, 4 * S_Q + BANKS)
            turned_high(3)
            squares()

            def q_copy(j):
                for b in range(BANKS):
                    act.wait_ge(bank_full, 4 * (S_Q + j) + b + 1)
                    act.activation(q_rows[:, b // 2, (b % 2) * HALF:(b % 2 + 1) * HALF], bank[:, b, :], ACT.Copy,
                                   scale=row_scale[:, 1, b // 2:b // 2 + 1]).then_inc(bank_free, 1)
                for f in range(4):
                    t, g = f // 2, f % 2
                    act.wait_ge(q_turned, 4 * j + f + 1)
                    act.activation(pact_hi[:, 4 * g:4 * g + 4, t * P:(t + 1) * P],
                                   misc[:, f, :].rearrange("p (c t) -> p c t", c=4), ACT.Copy).then_inc(q_hi, 1)

                for t in range(NB):
                    act.wait_ge(key_scores, NB * j + t + 1)
                    act.activation(scores[:, j, t, :], misc[:, 2 * t:2 * t + 2, :].rearrange("p b c -> p (b c)"), ACT.Copy)\
                        .then_inc(scores_copied, 1)

            tiles(first_tile(S_Q), LEAD, EARLY)
            root(3)
            tiles(first_tile(S_Q), LEAD + EARLY, KC - EARLY)
            act.wait_ge(scale_ready, 2)
            q_copy(0)
            tiles(first_tile(S_Q + 1), LEAD, KC - LEAD)
            q_copy(1)
            for first, last in ((0, NKEYS - SCORE_KEYS), (NKEYS - SCORE_KEYS, NKEYS)):
                if first:
                    act.wait_ge(topk_done, UNITS)
                    act.activation(gate[:, :, :], gate[:, :, :], ACT.Exp).then_inc(exp_done, 1)
                with act.Fori(first // BANKS, last // BANKS) as i:
                    for n in range(BANKS):
                        act.wait_ge(low_full, i * BANKS + (n + 1 + BANKS))
                        act.activation(plane[:, bass.ds(i * BANKS + n, 1), :].rearrange("p o t -> p (o t)"),
                                       bank[:, n, 0:SEQ], ACT.Copy).then_inc(low_copied, 1)
            def second_keys(rows_of, g, m, base, n_steps, first=0):
                act.wait_ge(hot_free, g + (base + 1))
                for n in range(first, GROUP):
                    i = act.activation(rows_of[:, m, n * P:(n + 1) * P], iota[:, :], ACT.Abs,
                                       bias=pick[:, 1, bass.ds(g * GROUP + n, 1)])
                i.then_inc(act_step, 1)
                act.wait_ge(act_step, g + (n_steps + base + 1))
                r = rows_of[:, m, first * P:]
                act.activation(r, r, ACT.Relu, bias=1.0, scale=-1.0).then_inc(second_ready, 1)

            def keys_copy(g, m):
                act.wait_ge(hot_free, g + 3)
                act.wait_ge(picked_full, g + 1)
                act.activation(keys_t[:, m, :], misc[:, m, :], ACT.Copy).then_inc(keys_copied, 1)

            act.wait_ge(picks_ready, 1)
            second_keys(second_bf, 0, 0, 0, step.n, POOL_TOKENS)
            with act.Fori(0, GROUPS // 2 - 1) as i:
                for m in range(2):
                    second_keys(second_bf, 2 * i + (m + 1), 1 - m, 0, step.n, POOL_TOKENS)
                    keys_copy(2 * i + m, m)
            second_keys(second_bf, GROUPS - 1, 1, 0, step.n, POOL_TOKENS)
            keys_copy(GROUPS - 2, 0)
            keys_copy(GROUPS - 1, 1)
            act.wait_ge(picked_full, 2 + GROUPS)
            second_keys(second_hot, 0, 0, GROUPS, step.n)
            act.wait_ge(dots_whole, 1)
            for b in range(NB):
                u = slice(b * PEER_HEADS, (b + 1) * PEER_HEADS)
                m = act.activation(weight[:, u, :], dots[:, u, :], ACT.Gelu, scale=row_scale[:, 1, b:b + 1])
            m.then_inc(gelu_done, 1)
            def spread_out(g, q):
                act.wait_ge(hot_free, g + (GROUPS + 3))
                act.activation(plane[:, :, bass.ds(g * GROUP, GROUP)], misc[:, q, :].rearrange("p (t k) -> p k t", t=GROUP),
                               ACT.Copy).then_inc(spread_copied, 1)

            with act.Fori(0, GROUPS // 4 - 1) as i:
                for q in range(4):
                    second_keys(second_hot, 4 * i + (q + 1), (q + 1) % 2, GROUPS, step.n)
                    spread_out(4 * i + q, q)
            for g in range(GROUPS - 4, GROUPS):
                if g + 1 < GROUPS:
                    second_keys(second_hot, g + 1, (g + 1) % 2, GROUPS, step.n)
                spread_out(g, g % 4)
            step.n += 2 * GROUPS
            act.wait_ge(spread_copied, 4 + GROUPS)
            with act.Fori(0, NKEYS // E_RING) as i:
                for r in range(E_RING):
                    act.wait_ge(e_free, i * E_RING + r + 1)
                    act.activation(staged[:, r, :], plane[:, bass.ds(i * E_RING + r, 1), :].rearrange("p o t -> p (o t)"),
                                   ACT.Copy).then_inc(staged_ready, 1)
            for b in range(NB):
                act.wait_ge(resid_ready, b + 1)
                step(act.activation(junk, x_sb[:, b, :], ACT.Square, accum_out=norm_a[:, b:b + 1]))
                act.sem_inc(squares_done, 1)
            root(4)
            act.wait_ge(final_weighted, NB)
            act.wait_ge(scale_ready, 3)
            act.activation(h2[:, 1, :], h2[:, 1, :], ACT.Copy, scale=row_scale[:, 2, 1:2]).then_inc(final_ready[1], 1)

        @block.vector
        def _(dve):
            dve.sem_inc(g_free, AHEAD + G_RING)
            dve.sem_inc(picked_read, 2)
            step = Steps(dve, dve_step)

            def tiles(t0, k0, n):
                for k in range(k0, k0 + n):
                    r = k % W_RING
                    dve.wait_ge(tile_hi, t0 + k + 1)
                    dve.tensor_tensor(w_lo[:, r, :], w_raw[:, r, :], w_hi[:, r, :].bitcast(F32), ALU.subtract)\
                        .then_inc(tile_lo, 1)

            def turned_low(stage):
                for f in range(8):
                    n = 8 * stage + f + 1
                    j, t, h = f // 4, (f // 2) % 2, f % 2
                    c = (j * SLAB + h * HALF) // P
                    dve.wait_ge(turned_hi, n)
                    dve.tensor_tensor(act_lo[:, c:c + 4, t * P:(t + 1) * P],
                                      misc[:, f % 4, :].rearrange("p (c t) -> p c t", c=4),
                                      act_hi[:, c:c + 4, t * P:(t + 1) * P].bitcast(F32), ALU.subtract)\
                        .then_inc(turned_lo, 1)

            def inverse_root(n, width):
                dve.wait_ge(root_done, n)
                a_, b_, c_ = norm_a[:, 0:width], norm_b[:, 0:width], norm_c[:, 0:width]
                step(dve.reciprocal(a_, c_))
                step(dve.tensor_tensor(c_, a_, a_, ALU.mult))
                step(dve.tensor_tensor(c_, c_, b_, ALU.mult))
                step(dve.tensor_scalar(c_, c_, -0.5, 1.5, ALU.mult, ALU.add))
                step(dve.tensor_tensor(a_, a_, c_, ALU.mult))

            def norm_factor(n, n_squares, which):
                dve.wait_ge(squares_done, n_squares)
                step(dve.tensor_scalar(norm_b[:, 0:NB], norm_a[:, 0:NB], 1.0 / D, EPS, ALU.mult, ALU.add))
                dve.sem_inc(norm_step, 1)
                inverse_root(n, NB)
                step(dve.tensor_copy(row_scale[:, which, :], norm_a[:, 0:NB]))
                dve.sem_inc(scale_ready, 1)

            dve.wait_ge(x_landed, 32)
            dve.wait_ge(norm1_landed, 16)
            for t in range(NB):
                dve.tensor_tensor(h_rows[:, t, :], x_sb[:, t, :], norm1, ALU.mult).then_inc(rows_ready, 1)
            norm_factor(1, 1, 0)
            tiles(0, 0, LEAD)
            turned_low(0)
            with dve.Fori(0, MIX_SLABS) as j:
                tiles(j * KC, LEAD, KC)
            dve.wait_ge(const_landed, CONSTS)
            for h in range(HEADS):
                dve.wait_ge(scores_full, h + 1)
                if h >= 2:
                    dve.wait_ge(y_full, h - 1)
                dve.tensor_tensor(probs[:, h % 2, 0:SEQ], misc[:, 2, 0:SEQ], mask[:, h, :], ALU.mult)
                dve.tensor_tensor(probs[:, h % 2, SEQ:SEQ + P], misc[:, 2, SEQ:SEQ + P], mask[:, h, 0:P], ALU.mult)\
                    .then_inc(probs_ready, 1)
            for f in range(POOL_GROUPS):
                dve.wait_ge(lin_hi, f + 1)
                for d in range(2):
                    c = 2 * f + d
                    m = dve.scalar_tensor_tensor(pact_lo[:, c, :], misc[:, f, d * SEQ:(d + 1) * SEQ], pscale[:, c:c + 1],
                                                 pact_hi[:, c, :].bitcast(F32), ALU.mult, ALU.subtract)
                m.then_inc(lin_lo, 1)
            t_gate = first_tile(S_GATE)
            tiles(t_gate, LEAD, EARLY)
            dve.wait_ge(y_copied, HEADS)
            for n in range(2 * HEADS):
                t, h = n // HEADS, n % HEADS
                m = dve.bn_stats(stat[:, n, :], rows[:, t, V0 + h * DV:V0 + (h + 1) * DV])
            step(m)
            for n in range(2 * HEADS):
                m = dve.bn_aggr(mean_var[:, n, :], stat[:, n, :])
            step(m)
            step(dve.tensor_scalar(norm_b[:, :], mean_var[:, :, 1], EPS, None, ALU.add))
            dve.sem_inc(norm_step, 1)
            tiles(t_gate, LEAD + EARLY, EARLY)
            inverse_root(2, 2 * HEADS)
            tiles(t_gate, LEAD + 2 * EARLY, 1)
            for t in range(NB):
                for h in range(HEADS):
                    y = rows[:, t, V0 + h * DV:V0 + (h + 1) * DV]
                    n = t * HEADS + h
                    m = dve.tensor_scalar(y, y, mean_var[:, n, 0:1], norm_a[:, n:n + 1], ALU.subtract, ALU.mult)
                m.then_inc(y_normed, 1)
            dve.memset(zeros[:, :], 0.0).then_inc(zeros_ready, 1)
            dve.wait_ge(keys_hi_done, 1)
            dve.tensor_tensor(keys_lo[:, :, :], keys_raw, keys_hi[:, :, :].bitcast(F32), ALU.subtract)\
                .then_inc(keys_split, 1)
            tiles(t_gate, LEAD + 2 * EARLY + 1, KC - 2 * EARLY - 1)
            with dve.Fori(1, GATE_SLABS) as j:
                tiles(j * KC + t_gate, LEAD, KC)
            turned_low(1)
            with dve.Fori(0, D_SLABS) as j:
                tiles(j * KC + first_tile(S_RET), LEAD, KC)
                for b in range(BANKS):
                    dve.wait_ge(bank_full, 4 * j + (4 * S_RET + b + 1))
                    g = rows[:, b // 2, bass.ds(j * SLAB + (b % 2) * HALF, HALF)]
                    dve.tensor_tensor(g, g, bank[:, b, :], ALU.mult).then_inc(bank_free, 1)
            with dve.Fori(0, D_SLABS) as j:
                tiles(j * POOL_KC + first_tile(S_POOL), LEAD, POOL_KC)
                for b in range(BANKS):
                    dve.wait_ge(bank_full, 4 * j + (4 * S_POOL + b + 1))
                    g = rows[:, b // 2, bass.ds(j * SLAB + (D + (b % 2) * HALF), HALF)]
                    dve.tensor_tensor(g, g, bank[:, b, :], ALU.mult).then_inc(bank_free, 1)
            turned_low(2)
            with dve.Fori(0, D_SLABS) as j:
                tiles(j * KC + first_tile(S_OUT), LEAD, KC)
                for b in range(BANKS):
                    dve.wait_ge(bank_full, 4 * j + (4 * S_OUT + b + 1))
                    g = x_sb[:, b // 2, bass.ds(j * SLAB + (b % 2) * HALF, HALF)]
                    dve.tensor_tensor(g, g, bank[:, b, :], ALU.add).then_inc(bank_free, 1)
            dve.wait_ge(bank_free, 4 * S_Q + BANKS)
            dve.wait_ge(norm2_landed, 16)
            dve.wait_ge(turned, 24)
            for t in range(NB):
                dve.tensor_tensor(h2[:, t, :], x_sb[:, t, :], norm2, ALU.mult).then_inc(rows_ready, 1)
            turned_low(3)

            def q_low(j):
                for f in range(4):
                    t, g = f // 2, f % 2
                    dve.wait_ge(q_hi, 4 * j + f + 1)
                    dve.tensor_tensor(pact_lo[:, 4 * g:4 * g + 4, t * P:(t + 1) * P],
                                      misc[:, f, :].rearrange("p (c t) -> p c t", c=4),
                                      pact_hi[:, 4 * g:4 * g + 4, t * P:(t + 1) * P].bitcast(F32), ALU.subtract)\
                        .then_inc(q_lo, 1)


            def two_rounds(st, pairs, work):
                for src, val, pos in pairs:
                    m = dve.max(val[:, 0:8], src)
                st(m)
                for src, val, pos in pairs:
                    dve.max_index(pos[:, 0:8], val[:, 0:8], src)
                for (src, val, pos), w in zip(pairs, work):
                    m = dve.match_replace(w, val[:, 0:8], src, NEG)
                st(m)
                for (src, val, pos), w in zip(pairs, work):
                    m = dve.max(val[:, 8:16], w)
                st(m)
                for (src, val, pos), w in zip(pairs, work):
                    m = dve.max_index(pos[:, 8:16], val[:, 8:16], w)
                st(m)

            left = list(range(LEAD, KC))

            def next_tile():
                if left:
                    tiles(first_tile(S_Q + 1), left.pop(0), 1)

            def top_experts(u):
                b, j, h = u // PEER_HEADS, (u % PEER_HEADS) // HEADS_PER_SLAB, u % HEADS_PER_SLAB
                st = step
                dve.wait_ge(scores_copied, NB * j + b + 1)
                s = scores[:, j, b, h * 2 * NKEYS:(h + 1) * 2 * NKEYS]
                two_rounds(st, [(s[:, p * NKEYS:(p + 1) * NKEYS], top_val[:, p, :], top_idx[:, p, :]) for p in range(2)],
                           [tmp_a[:, p * NKEYS:(p + 1) * NKEYS] for p in range(2)])
                next_tile()
                grid = [P, TOPK, TOPK]
                cand = tmp_b[:, 0:TOPK * TOPK]
                st(dve.tensor_tensor(cand.rearrange("p (a b) -> p a b", a=TOPK),
                                     top_val[:, 0, :].unsqueeze(2).to_broadcast(grid),
                                     top_val[:, 1, :].unsqueeze(1).to_broadcast(grid), ALU.add))
                two_rounds(st, [(cand, best[:, :], best_pos[:, :])], [tmp_a[:, 0:TOPK * TOPK]])
                next_tile()
                dve.tensor_scalar(gate[:, u, :], best[:, :], best[:, 0:1], None, ALU.subtract)
                dve.tensor_single_scalar(pos_ab[:, 0, :], best_pos[:, :], 4, ALU.logical_shift_right)
                st(dve.tensor_single_scalar(pos_ab[:, 1, :], best_pos[:, :], TOPK - 1, ALU.bitwise_and))
                hits = tmp_a[:, :].rearrange("p (h k j) -> p h k j", h=2, k=TOPK)
                for p in range(2):
                    m = dve.tensor_tensor(hits[:, p, :, :], pos_ab[:, p, :].unsqueeze(2).to_broadcast(grid),
                                          iota[:, 0:TOPK].unsqueeze(1).to_broadcast(grid), ALU.is_equal)
                st(m)
                for p in range(2):
                    m = dve.tensor_tensor(hits[:, p, :, :], hits[:, p, :, :],
                                          top_idx[:, p, :].unsqueeze(1).to_broadcast(grid), ALU.mult)
                st(m)
                st(dve.tensor_reduce(expert_ab[:, :, :], hits, AX_X, ALU.add))
                dve.scalar_tensor_tensor(expert[:, u, :], expert_ab[:, 0, :], float(NKEYS), expert_ab[:, 1, :],
                                         ALU.mult, ALU.add).then_inc(topk_done, 1)

            def dot_product(u, m, b, k, first=False):
                r = k % G_RING
                dve.wait_ge(g_landed[r], u * (16 * TOPK // G_RING) + 16 * (k // G_RING + 1))
                dve.tensor_tensor_reduce(out=g_ring[:, r, :], in0=g_ring[:, r, :], in1=h2[:, b, HALF_D:D], scale=1.0,
                                         scalar=0.0, op0=ALU.mult, op1=ALU.add,
                                         accum_out=dots_now[:, m, k:k + 1]).then_inc(g_free, 1)
                if k == 0 and not first:
                    dve.wait_ge(g_free, u * TOPK + (AHEAD + G_RING))
                    dve.tensor_copy(dots[:, bass.ds(u - 1, 1), :].rearrange("p u k -> p (u k)"), dots_now[:, 1 - m, :])

            tiles(first_tile(S_Q), LEAD, EARLY)
            norm_factor(3, 2, 1)
            tiles(first_tile(S_Q), LEAD + EARLY, KC - EARLY)
            q_low(0)
            top_experts(0)
            found = 1
            for u in range(PEER_HEADS):
                for k in range(TOPK):
                    dot_product(u, u % 2, 0, k, u == 0)
                    next_tile()
                    if (u, k) == (0, TOPK - 2):
                        q_low(1)
                    if found < UNITS and (k in (4, 12) and u or (u, k) == (0, 4)):
                        top_experts(found)
                        found += 1
            while found < UNITS:
                top_experts(found)
                found += 1
            dve.wait_ge(topk_done, UNITS)
            step(dve.tensor_copy(expert_f, expert[:, :, :].rearrange("p u k -> p (u k)")))
            dve.sem_inc(experts_flat, 1)
            with dve.Fori(PEER_HEADS // 2, (UNITS - PICK_UNITS) // 2) as i:
                for m in range(2):
                    for k in range(TOPK):
                        dot_product(2 * i + m, m, 1, k)
            def softmax_and_picks():
                dve.wait_ge(exp_done, 1)
                step(dve.tensor_reduce(gate_sum[:, 0, :], gate[:, :, :], AX_X, ALU.add))
                step(dve.reciprocal(gate_sum[:, 1, :], gate_sum[:, 0, :]))
                step(dve.tensor_tensor(gate[:, :, :], gate[:, :, :], gate_sum[:, 1, :].unsqueeze(2).to_broadcast([P, UNITS, TOPK]),
                                       ALU.mult))
                dve.wait_ge(experts_turned, 1)
                step(dve.tensor_copy(pick_int[:, 0, :], bank[:, 0, 0:SEQ]))
                dve.tensor_single_scalar(pick_int[:, 1, :], pick_int[:, 0, :], 7, ALU.logical_shift_right)
                step(dve.tensor_single_scalar(pick_int[:, 2, :], pick_int[:, 0, :], NKEYS - 1, ALU.bitwise_and))
                dve.tensor_single_scalar(pick[:, 1, :], pick_int[:, 2, :], -1.0, ALU.mult)
                step(dve.tensor_copy(pick[:, 0, :], pick_int[:, 1, :]))
                dve.sem_inc(picks_ready, 1)

            for i in range(PICK_UNITS * TOPK):
                u, k = UNITS - PICK_UNITS + i // TOPK, i % TOPK
                if i == PICK_UNITS * TOPK - PICK_DOTS:
                    softmax_and_picks()
                dot_product(u, u % 2, 1, k)
                for g in groups_at(i):
                    dve.wait_ge(picked_full, g + 3)
                    for n in range(GROUP):
                        t = g * GROUP + n
                        row = misc[:, 2 + g % 2, n * P:(n + 1) * P]
                        m = dve.scalar_tensor_tensor(row, iota[:, :], pick[:, 0, t:t + 1], row, ALU.is_equal, ALU.mult,
                                                     accum_out=low_dots[:, t:t + 1])
                    m.then_inc(picked_read, 1)
            dve.wait_ge(picked_read, 2 + GROUPS)
            dve.sem_inc(low_summed, 1)
            dve.wait_ge(dots_turned, 1)
            dve.wait_ge(g_free, AHEAD + G_RING + UNITS * TOPK)
            step(dve.tensor_copy(dots[:, UNITS - 1, :], dots_now[:, (UNITS - 1) % 2, :]))
            dots_flat = dots[:, :, :].rearrange("p u k -> p (u k)")
            dve.tensor_tensor(dots_flat, dots_flat, bank[:, 1, 0:SEQ], ALU.add).then_inc(dots_whole, 1)
            dve.wait_ge(gelu_done, 1)
            step(dve.tensor_tensor(weight[:, :, :], weight[:, :, :], gate[:, :, :], ALU.mult))
            dve.sem_inc(weighted, 1)
            dve.wait_ge(weights_turned, 1)
            dve.tensor_copy(pick[:, 2, :], bank[:, 2, 0:SEQ]).then_inc(weights_ready, 1)
            dve.wait_ge(weights_ready, 1)

            def add_row(u, b, k):
                r = k % G_RING
                acc = x_sb[:, b, HALF_D:D]
                dve.wait_ge(g_landed[r], (u + UNITS) * (16 * TOPK // G_RING) + 16 * (k // G_RING + 1))
                dve.wait_ge(g_free, (u + UNITS) * TOPK + (AHEAD + G_RING + k))
                dve.scalar_tensor_tensor(acc, g_ring[:, r, :], weight[:, bass.ds(u, 1), k:k + 1].rearrange("p u k -> p (u k)"),
                                         acc, ALU.mult, ALU.add).then_inc(g_free, 1)

            with dve.Fori(0, SPREAD_UNITS) as u:
                for k in range(TOPK):
                    g = u * TOPK + k
                    dve.wait_ge(hot_free, g + (GROUPS + 1))
                    for n in range(GROUP):
                        key, w = [pick[:, c, bass.ds(g * GROUP + n, 1)] for c in (0, 2)]
                        m = dve.tensor_scalar(first_hot[:, k % 2, n, :], iota[:, :], key, w, ALU.is_equal, ALU.mult)
                    m.then_inc(first_ready, 1)
                    add_row(u, 0, k)
            for first, last, b in ((SPREAD_UNITS, PEER_HEADS, 0), (PEER_HEADS, UNITS, 1)):
                with dve.Fori(first, last) as u:
                    for k in range(TOPK):
                        add_row(u, b, k)

            dve.wait_ge(y_peer_full, 1)
            dve.wait_ge(final_landed, 16)
            dve.wait_ge(g_free, AHEAD + G_RING + 2 * UNITS * TOPK)
            for b in range(NB):
                step(dve.tensor_tensor(x_sb[:, b, 0:D // 2], x_sb[:, b, 0:D // 2],
                                       bank[:, 2 * b:2 * b + 2, :].rearrange("p b c -> p (b c)"), ALU.add))
                dve.sem_inc(resid_ready, 1)
            for b in range(NB):
                dve.tensor_tensor(h2[:, b, :], x_sb[:, b, :], final_w[:, :], ALU.mult).then_inc(final_weighted, 1)
            norm_factor(4, 4, 2)
            dve.wait_ge(final_weighted, NB)
            dve.tensor_scalar(h2[:, 0, :], h2[:, 0, :], row_scale[:, 2, 0:1], None, ALU.mult).then_inc(final_ready[0], 1)

        @block.gpsimd
        def _(pool):
            step = Steps(pool, pool_step)
            ta = rope_tmp[:, 0:SLAB].rearrange("p (c f) -> p c f", f=DK // 2)
            tb = rope_tmp[:, SLAB:2 * SLAB].rearrange("p (h c f) -> p h c f", c=2, f=DK // 2)
            pool.wait_ge(const_landed, CONSTS)
            for n in range(2):
                pool.wait_ge(bank_free, 4 * (n + 1) + 4)
                for t in range(NB):
                    x = rows[:, t, n * Q_DIM:(n + 1) * Q_DIM]
                    xc = x.rearrange("p (c f) -> p c f", f=DK // 2)
                    xh = x.rearrange("p (h c f) -> p h c f", c=2, f=DK // 2)
                    th = rope_tmp[:, 0:SLAB].rearrange("p (h c f) -> p h c f", c=2, f=DK // 2)
                    full, part = [P, 2 * HEADS, DK // 2], [P, HEADS, DK // 2]
                    cos, sin = rope[:, t, 0, :].unsqueeze(1), rope[:, t, 1, :].unsqueeze(1)
                    pool.tensor_tensor(ta, xc, cos.to_broadcast(full), ALU.mult)
                    pool.tensor_tensor(tb[:, :, 0, :], xh[:, :, 1, :], sin.to_broadcast(part), ALU.mult)
                    step(pool.tensor_tensor(tb[:, :, 1, :], xh[:, :, 0, :], sin.to_broadcast(part), ALU.mult))
                    pool.tensor_tensor(xh[:, :, 0, :], th[:, :, 0, :], tb[:, :, 0, :], ALU.subtract)
                    step(pool.tensor_tensor(xh[:, :, 1, :], th[:, :, 1, :], tb[:, :, 1, :], ALU.add))
                    pool.sem_inc(rope_done, 1)
            pool.wait_ge(silu_done, NB)
            for t in range(NB):
                pool.wait_ge(y_normed, t + 1)
                pool.tensor_tensor(rows[:, t, G0:G0 + V_DIM], rows[:, t, G0:G0 + V_DIM], rows[:, t, V0:V0 + V_DIM], ALU.mult)\
                    .then_inc(ret_ready, 1)
            for f in range(8):
                j, t, h = f // 4, (f // 2) % 2, f % 2
                col = j * SLAB + h * HALF
                pool.wait_ge(bank_free, 4 * (S_POOL + 1) + f + 1)
                pool.tensor_tensor(rows[:, t, col:col + HALF], rows[:, t, col:col + HALF], rows[:, t, D + col:D + col + HALF],
                                   ALU.add).then_inc(mixed_ready, 1)

            def take_experts(u, m, e, wait_found):
                if wait_found:
                    pool.wait_ge(topk_done, e + 1)
                    pool.sem_inc(pool_passed, 1)
                pool.wait_ge(g_free, u * TOPK + G_RING)
                pool.sem_inc(pool_passed, 1)
                pool.tensor_copy(idx[:, m, :], expert[:, bass.ds(e, 1), :].rearrange("p u k -> p (u k)")).then_inc(idx_copied, 1)
                pool.wait_ge(idx_copied, u + 1)
                pool.sem_inc(pool_passed, 1)

            def gather(table, u, m, k):
                r = k % G_RING
                pool.wait_ge(g_free, u * TOPK + (AHEAD + k + 1))
                pool.sem_inc(pool_passed, 1)
                pool.indirect_dma_start(
                    out=g_ring[:, r, :], out_offset=None, in_=table,
                    in_offset=bass.IndirectOffsetOnAxis(ap=idx[:, m, k:k + 1], axis=0),
                ).then_inc(g_landed[r], 16)

            def units(table, first, last, e0, wait_found):
                with pool.Fori(0, (last - first) // 2) as i:
                    for m in range(2):
                        u = 2 * i + (m + first)
                        take_experts(u, m, 2 * i + (m + e0), wait_found)
                        for k in range(TOPK):
                            gather(table, u, m, k)

            def second_keys(g):
                pool.wait_ge(hot_free, g + 1)
                for n in range(POOL_TOKENS):
                    t = g * GROUP + n
                    m = pool.tensor_scalar(second_bf[:, g % 2, n * P:(n + 1) * P], iota[:, :], pick[:, 1, t:t + 1], 0.0,
                                           ALU.add, ALU.is_equal)
                m.then_inc(pool_ready, 1)

            pool.wait_ge(rows_ready, 2 * NB)
            first = UNITS - PICK_UNITS
            units(a["peer_u_up"], 0, first, 0, True)
            n = PICK_UNITS * TOPK
            for i in range(n + GATHERS_AHEAD):
                if i < n:
                    u, k = first + i // TOPK, i % TOPK
                    if k == 0:
                        take_experts(u, u % 2, u, True)
                    gather(a["peer_u_up"], u, u % 2, k)
                for g in groups_at(i - GATHERS_AHEAD):
                    if g == 0:
                        pool.wait_ge(picks_ready, 1)
                    second_keys(g)
            units(a["peer_v_up"], UNITS, 2 * UNITS, 0, False)


def kernel(x, norm1_w, w_in, w_ret_o, w_pool_lin, pool_scale, w_pool_o, w_out, norm2_w, peer_w_q,
           peer_sub_keys, peer_u, peer_v, final_norm_w):
    import concourse.bacc as bacc
    from concourse.bass_utils import run_bass_kernel_spmd

    host = {
        "x": x[0], "norm1_w": norm1_w[0], "w_in": w_in[0], "w_ret_o": w_ret_o[0], "w_pool_lin": w_pool_lin[0],
        "pool_scale": np.asarray(pool_scale)[0].reshape(POOL_KC, P).T,
        "w_pool_o": w_pool_o[0], "w_out": w_out[0], "norm2_w": norm2_w[0], "peer_w_q": peer_w_q[0],
        "peer_sub_keys": np.asarray(peer_sub_keys)[0].transpose(2, 0, 1).reshape(P, 2 * NKEYS),
        "peer_u_up": peer_u[0][:, HALF_D:], "peer_v_up": peer_v[0][:, HALF_D:],
        "peer_u_low": np.asarray(peer_u)[0][:, :HALF_D].reshape(NKEYS, NKEYS, LOW_KC, P).transpose(3, 0, 2, 1).reshape(P, -1),
        "peer_v": peer_v[0][:, :HALF_D], "final_norm_w": final_norm_w,
    }
    host.update(constants())
    nc = bacc.Bacc("TRN2", target_bir_lowering=False, num_devices=1)
    arrays, aps = {}, {}
    for name, value in host.items():
        value = np.ascontiguousarray(value)
        arrays[f"in_{name}"] = value
        aps[name] = nc.dram_tensor(f"in_{name}", value.shape, mybir.dt.from_np(value.dtype), kind="ExternalInput").ap()
    out = nc.dram_tensor("out_dram", (SEQ, D), F32, kind="ExternalOutput").ap()
    build(nc, aps, out)
    r = run_bass_kernel_spmd(nc, [arrays], core_ids=[0])
    return r.results[0]["out_dram"].reshape(1, SEQ, D)
```
